# Optimizing a Trainium2 kernel written in Bass

```python
import math
import jax, jax.numpy as jnp
from jax import lax
import numpy as np

D_MODEL = 1024
BATCH = 1
SEQ = 512
DEPTH = 1

CHUNK = 64
Q_BLOCK = 128
EPS = 1e-6
D_MIX = D_MODEL
M_HEADS = 4
M_WIDTH = D_MIX // 2
M_HEAD_DIM = M_WIDTH // M_HEADS
CONV_WIDTH = 4
A_HEADS = 4
A_WIDTH = D_MIX - M_WIDTH
A_HEAD_DIM = A_WIDTH // A_HEADS
A_QK_DIM = A_HEAD_DIM // 2
IN_SIZES = (2 * M_WIDTH, M_WIDTH, M_WIDTH, M_HEADS, M_HEADS, A_WIDTH, A_WIDTH, A_WIDTH)
IN_COLS = sum(IN_SIZES)
IN_SPLITS = tuple(int(s) for s in np.cumsum(IN_SIZES)[:-1])
N_GROUPS = 4
EXPERTS_PER_GROUP = 8
N_EXPERTS = N_GROUPS * EXPERTS_PER_GROUP
TOP_K = 2
D_EXPERT = D_MODEL // 2
MOE_BLOCK = 256


def rms_norm(x, w):
    xf = x.astype(jnp.float32)
    y = xf * lax.rsqrt(jnp.mean(xf * xf, axis=-1, keepdims=True) + EPS)
    return (y * w.astype(jnp.float32)).astype(x.dtype)

def causal_conv(x, w, b):
    S = x.shape[1]
    xp = jnp.pad(x, ((0, 0), (CONV_WIDTH - 1, 0), (0, 0)))
    out = b
    for j in range(CONV_WIDTH):
        out = out + xp[:, j:j + S] * w[j]
    return out

def mlstm_chunkwise(q, k, v, i_pre, f_pre):
    Bn, S, H, Dh = q.shape
    NC = S // CHUNK

    def to_chunks(t):
        t = t.astype(jnp.float32).reshape((Bn, NC, CHUNK) + t.shape[2:])
        return jnp.moveaxis(jnp.moveaxis(t, 1, 0), 3, 2)

    qc = to_chunks(q)
    kc = to_chunks(k) * (Dh ** -0.5)
    vc = to_chunks(v)
    ic = to_chunks(i_pre)
    fc = jax.nn.log_sigmoid(to_chunks(f_pre))
    causal = jnp.tril(jnp.ones((CHUNK, CHUNK), dtype=bool))

    def step(carry, inp):
        C, n, m = carry
        q_c, k_c, v_c, i_c, lf_c = inp
        b = jnp.cumsum(lf_c, axis=-1)
        log_d = jnp.where(causal, b[..., :, None] - b[..., None, :] + i_c[..., None, :], -jnp.inf)
        log_inter = b + m[..., None]
        m_t = jnp.maximum(log_inter, jnp.max(log_d, axis=-1))
        d = jnp.exp(log_d - m_t[..., None])
        inter = jnp.exp(log_inter - m_t)
        s = jnp.einsum('bhtd,bhsd->bhts', q_c, k_c) * d
        num = jnp.einsum('bhts,bhse->bhte', s, v_c) + inter[..., None] * jnp.einsum('bhtd,bhde->bhte', q_c, C)
        den = jnp.sum(s, axis=-1) + inter * jnp.einsum('bhtd,bhd->bht', q_c, n)
        h = num / jnp.maximum(jnp.abs(den), jnp.exp(-m_t))[..., None]
        b_end = b[..., -1]
        log_w = b_end[..., None] - b + i_c
        m_new = jnp.maximum(b_end + m, jnp.max(log_w, axis=-1))
        w = jnp.exp(log_w - m_new[..., None])
        decay = jnp.exp(b_end + m - m_new)
        C_new = decay[..., None, None] * C + jnp.einsum('bhs,bhsd,bhse->bhde', w, k_c, v_c)
        n_new = decay[..., None] * n + jnp.einsum('bhs,bhsd->bhd', w, k_c)
        return (C_new, n_new, m_new), h

    init = (jnp.zeros((Bn, H, Dh, Dh), jnp.float32),
            jnp.zeros((Bn, H, Dh), jnp.float32),
            jnp.zeros((Bn, H), jnp.float32))
    _, h = lax.scan(step, init, (qc, kc, vc, ic, fc))
    h = jnp.moveaxis(jnp.moveaxis(h, 0, 1), 2, 3)
    return h.reshape(Bn, S, H, Dh)

def diff_attention(q, k, v, q_norm_w, k_norm_w, lq1, lk1, lq2, lk2, a_norm_w, lambda_init):
    Bn, S = q.shape[:2]
    NQ = S // Q_BLOCK
    q = rms_norm(q, q_norm_w)
    k = rms_norm(k, k_norm_w)
    f32 = jnp.float32
    lam = (jnp.exp(jnp.sum(lq1.astype(f32) * lk1.astype(f32)))
           - jnp.exp(jnp.sum(lq2.astype(f32) * lk2.astype(f32))) + lambda_init)
    kt = jnp.transpose(k, (0, 2, 3, 1, 4))
    vt = jnp.transpose(v, (0, 2, 1, 3))
    qb = q.reshape(Bn, NQ, Q_BLOCK, A_HEADS, 2, A_QK_DIM).transpose(1, 0, 3, 4, 2, 5)
    key_chunk = jnp.arange(S) // CHUNK
    scale = A_QK_DIM ** -0.5

    def block(args):
        q_blk, idx = args
        q_chunk = (idx * Q_BLOCK + jnp.arange(Q_BLOCK)) // CHUNK
        mask = key_chunk[None, :] <= q_chunk[:, None]
        s = jnp.einsum('bhcqd,bhcsd->bhcqs', q_blk, kt).astype(f32) * scale
        p = jax.nn.softmax(jnp.where(mask, s, -jnp.inf), axis=-1)
        attn = p[:, :, 0] - lam * p[:, :, 1]
        return jnp.einsum('bhqs,bhsd->bhqd', attn.astype(v.dtype), vt)

    o = lax.map(block, (qb, jnp.arange(NQ)))
    o = o.transpose(1, 0, 3, 2, 4).reshape(Bn, S, A_HEADS, A_HEAD_DIM)
    o = rms_norm(o, a_norm_w) * (1.0 - lambda_init)
    return o.reshape(Bn, S, A_WIDTH)

def hybrid_mixer(h, w_in, b_igate, b_fgate, conv_w, conv_b, m_norm_w, q_norm_w, k_norm_w,
                 lq1, lk1, lq2, lk2, a_norm_w, w_out, lambda_init):
    Bn, S, _ = h.shape
    proj = h @ w_in
    mqk, mv, mo, mi, mf, aq, ak, av = jnp.split(proj, IN_SPLITS, axis=-1)
    qk = jax.nn.silu(causal_conv(mqk, conv_w, conv_b))
    mq, mk = jnp.split(qk, 2, axis=-1)
    shp = (Bn, S, M_HEADS, M_HEAD_DIM)
    hm = mlstm_chunkwise(mq.reshape(shp), mk.reshape(shp), mv.reshape(shp), mi + b_igate, mf + b_fgate)
    hm = jax.nn.sigmoid(mo).reshape(shp) * hm.astype(h.dtype)
    hm = rms_norm(hm, m_norm_w).reshape(Bn, S, M_WIDTH)
    ha = diff_attention(aq.reshape(Bn, S, A_HEADS, 2, A_QK_DIM), ak.reshape(Bn, S, A_HEADS, 2, A_QK_DIM),
                        av.reshape(Bn, S, A_HEADS, A_HEAD_DIM), q_norm_w, k_norm_w,
                        lq1, lk1, lq2, lk2, a_norm_w, lambda_init)
    return jnp.concatenate([hm, ha], axis=-1) @ w_out

def hierarchical_moe(h, w_group, b_group, w_expert, b_expert, w_gate, w_up, w_down):
    Bn, S, D = h.shape
    T = Bn * S
    xt = h.reshape(T, D)
    f32 = jnp.float32
    g_logits = (xt @ w_group).astype(f32) + b_group.astype(f32)
    g_prob = jax.nn.softmax(g_logits, axis=-1)
    g_sel = jnp.argmax(g_logits, axis=-1)
    g_w = jnp.take_along_axis(g_prob, g_sel[:, None], axis=1)[:, 0]
    e_logits = ((xt @ w_expert).astype(f32) + b_expert.astype(f32)).reshape(T, N_GROUPS, EXPERTS_PER_GROUP)
    e_in = jnp.take_along_axis(e_logits, g_sel[:, None, None], axis=1)[:, 0]
    top_vals, top_idx = lax.top_k(e_in, TOP_K)
    weights = g_w[:, None] * jax.nn.softmax(top_vals, axis=-1)
    eid = (g_sel[:, None] * EXPERTS_PER_GROUP + top_idx).reshape(-1)
    A = T * TOP_K
    tok = jnp.arange(A) // TOP_K
    counts = jax.ops.segment_sum(jnp.ones_like(eid), eid, num_segments=N_EXPERTS)
    padded = ((counts + MOE_BLOCK - 1) // MOE_BLOCK) * MOE_BLOCK
    pad_end = jnp.cumsum(padded)
    pad_start = pad_end - padded
    start = jnp.cumsum(counts) - counts
    order = jnp.argsort(eid)
    eid_sorted = eid[order]
    dest_sorted = pad_start[eid_sorted] + (jnp.arange(A) - start[eid_sorted])
    dest = jnp.zeros((A,), jnp.int32).at[order].set(dest_sorted.astype(jnp.int32))
    P = ((A + MOE_BLOCK - 1) // MOE_BLOCK) * MOE_BLOCK + N_EXPERTS * MOE_BLOCK
    NB = P // MOE_BLOCK
    block_start = jnp.arange(NB) * MOE_BLOCK
    block_expert = jnp.minimum(jnp.sum(pad_end[None, :] <= block_start[:, None], axis=1), N_EXPERTS - 1)
    x_buf = jnp.zeros((P, D), h.dtype).at[dest].set(xt[tok])

    def expert_block(args):
        xb, e = args
        hid = jax.nn.silu(xb @ w_gate[e]) * (xb @ w_up[e])
        return hid @ w_down[e]

    y_buf = lax.map(expert_block, (x_buf.reshape(NB, MOE_BLOCK, D), block_expert)).reshape(P, D)
    y = jnp.sum(y_buf[dest].reshape(T, TOP_K, D) * weights[..., None].astype(h.dtype), axis=1)
    return y.reshape(Bn, S, D)

def first_inputs(seed: int = 0) -> dict:
    key = jax.random.key(seed)
    ks = jax.random.split(key, 24)
    nrm = jax.random.normal
    f32 = jnp.float32
    L = DEPTH
    gain = lambda k, n: 1.0 + 0.01 * nrm(k, (L, n), f32)
    return {
        'x': nrm(ks[0], (BATCH, SEQ, D_MODEL), f32),
        'norm1_w': gain(ks[1], D_MODEL),
        'w_in': nrm(ks[2], (L, D_MODEL, IN_COLS), f32) * D_MODEL ** -0.5,
        'b_igate': 0.1 * nrm(ks[3], (L, M_HEADS), f32),
        'b_fgate': jnp.linspace(3.0, 6.0, M_HEADS, dtype=f32)[None, :] + 0.1 * nrm(ks[4], (L, M_HEADS), f32),
        'conv_w': nrm(ks[5], (L, CONV_WIDTH, 2 * M_WIDTH), f32) * CONV_WIDTH ** -0.5,
        'conv_b': 0.01 * nrm(ks[6], (L, 2 * M_WIDTH), f32),
        'm_norm_w': gain(ks[7], M_HEAD_DIM),
        'q_norm_w': gain(ks[8], A_QK_DIM),
        'k_norm_w': gain(ks[9], A_QK_DIM),
        'lambda_q1': 0.1 * nrm(ks[10], (L, A_QK_DIM), f32),
        'lambda_k1': 0.1 * nrm(ks[11], (L, A_QK_DIM), f32),
        'lambda_q2': 0.1 * nrm(ks[12], (L, A_QK_DIM), f32),
        'lambda_k2': 0.1 * nrm(ks[13], (L, A_QK_DIM), f32),
        'a_norm_w': gain(ks[14], A_HEAD_DIM),
        'w_out': nrm(ks[15], (L, D_MIX, D_MODEL), f32) * D_MIX ** -0.5,
        'norm2_w': gain(ks[16], D_MODEL),
        'w_group': nrm(ks[17], (L, D_MODEL, N_GROUPS), f32) * D_MODEL ** -0.5,
        'b_group': 0.01 * nrm(ks[18], (L, N_GROUPS), f32),
        'w_expert': nrm(ks[19], (L, D_MODEL, N_EXPERTS), f32) * D_MODEL ** -0.5,
        'b_expert': 0.01 * nrm(ks[20], (L, N_EXPERTS), f32),
        'w_gate': nrm(ks[21], (L, N_EXPERTS, D_MODEL, D_EXPERT), f32) * D_MODEL ** -0.5,
        'w_up': nrm(ks[22], (L, N_EXPERTS, D_MODEL, D_EXPERT), f32) * D_MODEL ** -0.5,
        'w_down': nrm(ks[23], (L, N_EXPERTS, D_EXPERT, D_MODEL), f32) * D_EXPERT ** -0.5,
    }

def first_block(x, norm1_w, w_in, b_igate, b_fgate, conv_w, conv_b, m_norm_w, q_norm_w, k_norm_w,
              lambda_q1, lambda_k1, lambda_q2, lambda_k2, a_norm_w, w_out, norm2_w,
              w_group, b_group, w_expert, b_expert, w_gate, w_up, w_down):
    for l in range(DEPTH):
        lambda_init = 0.8 - 0.6 * math.exp(-0.3 * l)
        h = rms_norm(x, norm1_w[l])
        x = x + hybrid_mixer(h, w_in[l], b_igate[l], b_fgate[l], conv_w[l], conv_b[l], m_norm_w[l],
                             q_norm_w[l], k_norm_w[l], lambda_q1[l], lambda_k1[l], lambda_q2[l],
                             lambda_k2[l], a_norm_w[l], w_out[l], lambda_init)
        h = rms_norm(x, norm2_w[l])
        x = x + hierarchical_moe(h, w_group[l], b_group[l], w_expert[l], b_expert[l],
                                 w_gate[l], w_up[l], w_down[l])
    return x


GRID_W = 64
CTX_LEN = 256
D_HYENA = 512
D_GLA = D_MODEL - D_HYENA
GLA_HEADS = 4
GLA_DK = D_GLA // 2
GLA_DV = D_GLA
GLA_HEAD_DK = GLA_DK // GLA_HEADS
GLA_HEAD_DV = GLA_DV // GLA_HEADS
GATE_RANK = 16
GATE_NORMALIZER = 16.0
GLA_CHUNK = 64
SHORT_CONV = 3
FILTER_EMB = 33
FILTER_BANDS = (FILTER_EMB - 1) // 2
FILTER_HIDDEN = 64
FAST_DECAY_PCT = 0.3
SLOW_DECAY_PCT = 1.5
DECAY_TARGET = 1e-2
D_FF = 4 * D_MODEL
PROJ_WIDTHS = (3 * D_HYENA, GLA_DK, GLA_DK, GLA_DV, GLA_DV, GATE_RANK, GATE_RANK)
PROJ_SPLITS = tuple(int(s) for s in np.cumsum(PROJ_WIDTHS)[:-1])
N_IN = sum(PROJ_WIDTHS)


def _rms_norm(x, g):
    xf = x.astype(jnp.float32)
    y = xf * lax.rsqrt(jnp.mean(xf * xf, axis=-1, keepdims=True) + EPS)
    return (y * g.astype(jnp.float32)).astype(x.dtype)

def _sq_relu_mlp(h, w1, w2):
    return jnp.square(jax.nn.relu(h @ w1)) @ w2

def _short_conv(u, w, b):
    t = u.shape[-2]
    pad = SHORT_CONV // 2
    up = jnp.pad(u, [(0, 0)] * (u.ndim - 2) + [(pad, pad), (0, 0)])
    out = b
    for j in range(SHORT_CONV):
        out = out + w[j] * up[..., j:j + t, :]
    return out

def _hyena_spectrum(length, w1, b1, w2, b2, w3, b3, freq, wout):
    f32 = jnp.float32
    t = jnp.linspace(0.0, 1.0, length, dtype=f32)[:, None]
    w = 2.0 * math.pi * jnp.arange(length, dtype=f32) / length
    f = jnp.linspace(1e-4, FILTER_BANDS - 1, FILTER_BANDS, dtype=f32)
    ang = w[:, None] * f[None, :]
    z = jnp.concatenate([t, jnp.cos(ang), -jnp.sin(ang)], axis=-1)
    fr = freq.astype(f32)
    hdn = jnp.sin(fr * (z @ w1.astype(f32) + b1.astype(f32)))
    hdn = jnp.sin(fr * (hdn @ w2.astype(f32) + b2.astype(f32)))
    hdn = jnp.sin(fr * (hdn @ w3.astype(f32) + b3.astype(f32)))
    h = (hdn @ wout.astype(f32)).reshape(length, 2, D_HYENA)
    min_decay = math.log(DECAY_TARGET) / SLOW_DECAY_PCT
    max_decay = math.log(DECAY_TARGET) / FAST_DECAY_PCT
    deltas = jnp.abs(jnp.linspace(min_decay, max_decay, D_HYENA, dtype=f32))
    h = h * jnp.exp(-t * deltas)[:, None, :]
    kern = jnp.concatenate([h[:, 0], jnp.zeros((1, D_HYENA), f32), h[:0:-1, 1]], axis=0)
    kern = kern * lax.rsqrt(jnp.sum(kern * kern, axis=0, keepdims=True) + EPS)
    return jnp.fft.rfft(kern, axis=0)

def _long_conv(u, spec, bias):
    length = u.shape[1]
    uf = u.astype(jnp.float32)
    y = jnp.fft.irfft(jnp.fft.rfft(uf, n=2 * length, axis=1) * spec, n=2 * length, axis=1)[:, :length]
    return (y + uf * bias.astype(jnp.float32)).astype(u.dtype)

def _hyena_gate_conv(u, spec, bias):
    x0, x1, v = jnp.split(u, 3, axis=-1)
    return x0 * _long_conv(x1 * v, spec, bias)

def _to_heads(z, n_heads):
    b, t, w = z.shape
    return z.reshape(b, t, n_heads, w // n_heads).transpose(0, 2, 1, 3)

def _log_gate(gr, w, b):
    lg = jax.nn.log_sigmoid(gr.astype(jnp.float32) @ w.astype(jnp.float32) + b.astype(jnp.float32))
    return _to_heads(lg / GATE_NORMALIZER, GLA_HEADS)

def _gla_chunked(q, k, v, lg, s0):
    bsz, nh, t, dk = q.shape
    dv = v.shape[-1]
    n = t // GLA_CHUNK
    q = q.reshape(bsz, nh, n, GLA_CHUNK, dk)
    k = k.reshape(bsz, nh, n, GLA_CHUNK, dk)
    lg = lg.reshape(bsz, nh, n, GLA_CHUNK, dk)
    v = v.reshape(bsz, nh, n, GLA_CHUNK, dv)
    b = jnp.cumsum(lg, axis=3)
    b_last = b[:, :, :, -1:, :]
    q_in = q * jnp.exp(b)
    k_in = k * jnp.exp(-b)
    k_end = k * jnp.exp(b_last - b)
    mask = jnp.tril(jnp.ones((GLA_CHUNK, GLA_CHUNK), dtype=bool))
    att = jnp.where(mask, jnp.einsum('bhncd,bhnsd->bhncs', q_in, k_in), 0.0)
    o_intra = jnp.einsum('bhncs,bhnse->bhnce', att, v)
    ds = jnp.einsum('bhnsd,bhnse->nbhde', k_end, v)
    decay = jnp.moveaxis(jnp.exp(b_last[:, :, :, 0, :]), 2, 0)

    def step(s, inp):
        d, dsn = inp
        return d[..., None] * s + dsn, s

    s_final, s_start = lax.scan(step, s0, (decay, ds))
    o_inter = jnp.einsum('bhncd,nbhde->bhnce', q_in, s_start)
    return (o_intra + o_inter).reshape(bsz, nh, t, dv), s_final

def _gla_final_state(k, v, lg):
    b = jnp.cumsum(lg, axis=2)
    return jnp.einsum('bhtd,bhte->bhde', k * jnp.exp(b[:, :, -1:] - b), v)

def _rev(a):
    return jnp.flip(a, axis=2)

def _gla_bidir(q, k, v, lg_f, lg_b, s_f0, s_b0):
    o_f, s_f = _gla_chunked(q, k, v, lg_f, s_f0)
    o_b, s_b = _gla_chunked(_rev(q), _rev(k), _rev(v), _rev(lg_b), s_b0)
    return o_f + _rev(o_b), s_f, s_b

def _gla_heads(q, k, v):
    f32 = jnp.float32
    qh = _to_heads(q.astype(f32), GLA_HEADS) * (GLA_HEAD_DK ** -0.5)
    return qh, _to_heads(k.astype(f32), GLA_HEADS), _to_heads(v.astype(f32), GLA_HEADS)

def _gla_output(o, og, g_norm):
    on = o * lax.rsqrt(jnp.mean(o * o, axis=-1, keepdims=True) + EPS) * g_norm.astype(jnp.float32)
    bsz, _, t, _ = o.shape
    y = on.transpose(0, 2, 1, 3).reshape(bsz, t, GLA_DV)
    return (y * jax.nn.silu(og.astype(jnp.float32))).astype(og.dtype)

def second_inputs(seed: int = 0) -> dict:
    key = jax.random.key(seed)
    ks = jax.random.split(key, 29)
    D = D_MODEL
    L = DEPTH

    def nrm(i, shape, scale):
        return scale * jax.random.normal(ks[i], shape, jnp.float32)

    return {
        'x': nrm(0, (BATCH, SEQ, D), 1.0),
        'c': nrm(1, (BATCH, D), 1.0),
        'ctx': nrm(2, (BATCH, CTX_LEN, D), 1.0),
        'c_ctx': nrm(3, (D,), 1.0),
        'w_ada': nrm(4, (L, D, 6 * D), 0.5 * D ** -0.5),
        'b_ada': nrm(5, (L, 6 * D), 0.02),
        'norm_mix': 1.0 + nrm(6, (L, D), 0.05),
        'norm_mlp': 1.0 + nrm(7, (L, D), 0.05),
        'w_in': nrm(8, (L, D, N_IN), D ** -0.5),
        'conv_w': nrm(9, (L, SHORT_CONV, 3 * D_HYENA), SHORT_CONV ** -0.5),
        'conv_b': nrm(10, (L, 3 * D_HYENA), 0.02),
        'filt_w1': nrm(11, (L, FILTER_EMB, FILTER_HIDDEN), FILTER_EMB ** -0.5),
        'filt_b1': nrm(12, (L, FILTER_HIDDEN), 0.1),
        'filt_w2': nrm(13, (L, FILTER_HIDDEN, FILTER_HIDDEN), FILTER_HIDDEN ** -0.5),
        'filt_b2': nrm(14, (L, FILTER_HIDDEN), 0.1),
        'filt_w3': nrm(15, (L, FILTER_HIDDEN, FILTER_HIDDEN), FILTER_HIDDEN ** -0.5),
        'filt_b3': nrm(16, (L, FILTER_HIDDEN), 0.1),
        'filt_freq': 1.0 + nrm(17, (L, FILTER_HIDDEN), 0.1),
        'filt_wout': nrm(18, (L, FILTER_HIDDEN, 2 * D_HYENA), FILTER_HIDDEN ** -0.5),
        'hyena_bias': nrm(19, (L, D_HYENA), 0.5),
        'gk_w_fwd': nrm(20, (L, GATE_RANK, GLA_DK), GATE_RANK ** -0.5),
        'gk_b_fwd': nrm(21, (L, GLA_DK), 0.1),
        'gk_w_bwd': nrm(22, (L, GATE_RANK, GLA_DK), GATE_RANK ** -0.5),
        'gk_b_bwd': nrm(23, (L, GLA_DK), 0.1),
        'gla_norm': 1.0 + nrm(24, (L, GLA_HEAD_DV), 0.05),
        'w_out': nrm(25, (L, D, D), D ** -0.5),
        'w_mlp1': nrm(26, (L, D, D_FF), D ** -0.5),
        'w_mlp2': nrm(27, (L, D_FF, D), D_FF ** -0.5),
        'norm_final': 1.0 + nrm(28, (D,), 0.05),
    }

def second_block(x, c, ctx, c_ctx, w_ada, b_ada, norm_mix, norm_mlp, w_in, conv_w, conv_b,
              filt_w1, filt_b1, filt_w2, filt_b2, filt_w3, filt_b3, filt_freq, filt_wout,
              hyena_bias, gk_w_fwd, gk_b_fwd, gk_w_bwd, gk_b_bwd, gla_norm, w_out,
              w_mlp1, w_mlp2, norm_final):
    bsz, seq, _ = x.shape
    rows = seq // GRID_W
    ctx_len = ctx.shape[1]
    for l in range(DEPTH):
        last = l == DEPTH - 1
        filt = (filt_w1[l], filt_b1[l], filt_w2[l], filt_b2[l], filt_w3[l], filt_b3[l], filt_freq[l], filt_wout[l])
        mod = jax.nn.silu(c) @ w_ada[l] + b_ada[l]
        mod_c = jax.nn.silu(c_ctx) @ w_ada[l] + b_ada[l]
        sh1, sc1, g1, sh2, sc2, g2 = jnp.split(mod[:, None, :], 6, axis=-1)
        csh1, csc1, cg1, csh2, csc2, cg2 = jnp.split(mod_c, 6)

        h_lat = _rms_norm(x, norm_mix[l]) * (1.0 + sc1) + sh1
        h_ctx = _rms_norm(ctx, norm_mix[l]) * (1.0 + csc1) + csh1
        hy_l, q_l, k_l, v_l, og_l, gf_l, gb_l = jnp.split(h_lat @ w_in[l], PROJ_SPLITS, axis=-1)
        hy_c, q_c, k_c, v_c, og_c, gf_c, gb_c = jnp.split(h_ctx @ w_in[l], PROJ_SPLITS, axis=-1)

        qh_c, kh_c, vh_c = _gla_heads(q_c, k_c, v_c)
        lgf_c = _log_gate(gf_c, gk_w_fwd[l], gk_b_fwd[l])
        lgb_c = _log_gate(gb_c, gk_w_bwd[l], gk_b_bwd[l])
        if last:
            s_f = _gla_final_state(kh_c, vh_c, lgf_c)
            s_b = _gla_final_state(_rev(kh_c), _rev(vh_c), _rev(lgb_c))
        else:
            zeros = jnp.zeros((bsz, GLA_HEADS, GLA_HEAD_DK, GLA_HEAD_DV), jnp.float32)
            o_c, s_f, s_b = _gla_bidir(qh_c, kh_c, vh_c, lgf_c, lgb_c, zeros, zeros)

        qh_l, kh_l, vh_l = _gla_heads(q_l, k_l, v_l)
        lgf_l = _log_gate(gf_l, gk_w_fwd[l], gk_b_fwd[l])
        lgb_l = _log_gate(gb_l, gk_w_bwd[l], gk_b_bwd[l])
        o_l, _, _ = _gla_bidir(qh_l, kh_l, vh_l, lgf_l, lgb_l, s_f, s_b)
        y_gla_l = _gla_output(o_l, og_l, gla_norm[l])

        u_l = _short_conv(hy_l.reshape(bsz, rows, GRID_W, 3 * D_HYENA), conv_w[l], conv_b[l])
        u_l = u_l.reshape(bsz, seq, 3 * D_HYENA)
        y_hy_l = _hyena_gate_conv(u_l, _hyena_spectrum(seq, *filt), hyena_bias[l])

        x = x + g1 * (jnp.concatenate([y_hy_l, y_gla_l], axis=-1) @ w_out[l])
        h2 = _rms_norm(x, norm_mlp[l]) * (1.0 + sc2) + sh2
        x = x + g2 * _sq_relu_mlp(h2, w_mlp1[l], w_mlp2[l])

        if not last:
            u_c = _short_conv(hy_c, conv_w[l], conv_b[l])
            y_hy_c = _hyena_gate_conv(u_c, _hyena_spectrum(ctx_len, *filt), hyena_bias[l])
            y_gla_c = _gla_output(o_c, og_c, gla_norm[l])
            ctx = ctx + cg1 * (jnp.concatenate([y_hy_c, y_gla_c], axis=-1) @ w_out[l])
            h2c = _rms_norm(ctx, norm_mlp[l]) * (1.0 + csc2) + csh2
            ctx = ctx + cg2 * _sq_relu_mlp(h2c, w_mlp1[l], w_mlp2[l])
    return _rms_norm(x, norm_final)


def setup_inputs(seed=0):
    out = dict(first_inputs(seed))
    for name, value in second_inputs(seed + 1).items():
        if name != "x":
            out[name + "_2"] = value
    return out


def reference(
    x, norm1_w, w_in, b_igate, b_fgate, conv_w, conv_b, m_norm_w, q_norm_w, k_norm_w, lambda_q1,
    lambda_k1, lambda_q2, lambda_k2, a_norm_w, w_out, norm2_w, w_group, b_group, w_expert,
    b_expert, w_gate, w_up, w_down, c_2, ctx_2, c_ctx_2, w_ada_2, b_ada_2, norm_mix_2,
    norm_mlp_2, w_in_2, conv_w_2, conv_b_2, filt_w1_2, filt_b1_2, filt_w2_2, filt_b2_2,
    filt_w3_2, filt_b3_2, filt_freq_2, filt_wout_2, hyena_bias_2, gk_w_fwd_2, gk_b_fwd_2,
    gk_w_bwd_2, gk_b_bwd_2, gla_norm_2, w_out_2, w_mlp1_2, w_mlp2_2, norm_final_2,
):
    x = first_block(
        x, norm1_w, w_in, b_igate, b_fgate, conv_w, conv_b, m_norm_w, q_norm_w, k_norm_w,
        lambda_q1, lambda_k1, lambda_q2, lambda_k2, a_norm_w, w_out, norm2_w, w_group, b_group,
        w_expert, b_expert, w_gate, w_up, w_down,
    )
    return second_block(
        x, c_2, ctx_2, c_ctx_2, w_ada_2, b_ada_2, norm_mix_2, norm_mlp_2, w_in_2, conv_w_2,
        conv_b_2, filt_w1_2, filt_b1_2, filt_w2_2, filt_b2_2, filt_w3_2, filt_b3_2, filt_freq_2,
        filt_wout_2, hyena_bias_2, gk_w_fwd_2, gk_b_fwd_2, gk_w_bwd_2, gk_b_bwd_2, gla_norm_2,
        w_out_2, w_mlp1_2, w_mlp2_2, norm_final_2,
    )


_drawn_inputs = setup_inputs


def setup_inputs(seed=0):
    import zlib

    import numpy as np

    out = dict(_drawn_inputs(seed))
    spreads = {}
    factors = {'b_igate': 64.0,
     'conv_b': 4.113,
     'm_norm_w': 3.022,
     'q_norm_w': 5.212,
     'k_norm_w': 4.299,
     'lambda_q1': 4.993,
     'a_norm_w': 3.586,
     'norm2_w': 3.468,
     'b_group': 5.609,
     'b_expert': 4.018,
     'ctx_2': 5.178,
     'c_ctx_2': 6.718,
     'norm_mlp_2': 20.085,
     'conv_b_2': 20.797,
     'gk_w_fwd_2': 3.276,
     'gk_b_fwd_2': 8.0,
     'gk_w_bwd_2': 3.329,
     'gk_b_bwd_2': 8.0,
     'gla_norm_2': 54.879,
     'norm_mix_2': 2.826,
     'filt_b1_2': 8.0,
     'filt_b2_2': 4.702,
     'filt_b3_2': 4.83,
     'filt_freq_2': 8.0}
    for name, (base, spread) in spreads.items():
        noise = np.random.default_rng([zlib.crc32(name.encode()), seed]).standard_normal(out[name].shape)
        drawn = base * np.exp(spread * noise) if base else spread * noise
        out[name] = __import__('jax').numpy.asarray(drawn.astype(out[name].dtype))
    for name, factor in factors.items():
        out[name] = (out[name] * factor).astype(out[name].dtype)
    return out
```

```python
from contextlib import ExitStack

import numpy as np
import concourse.bass as bass
from concourse import mybir

F32 = mybir.dt.float32
I32 = mybir.dt.int32
U32 = mybir.dt.uint32
ALU = mybir.AluOpType
ACT = mybir.ActivationFunctionType
AX = mybir.AxisListType

P = 128
D = 1024
KD = D // P
T = 512
TT = T // P
CW = 512
SLOTS = 6
HEADS = 4
HD = 128
NE = 32
EG = 8
NG = 4
FE = 512
BS = 64
SB_ = T // BS
EPS = 1e-6
BIG = 1e30
CTX = 256
DFF = 4096
LAMBDA_INIT = 0.8 - 0.6
CHUNK = 64

COLS = {}
_n = 0
for _name, _w in (("norm1", 8), ("conv_w", 32), ("conv_b", 8), ("m_norm", 1), ("a_norm", 1), ("q_norm", 1),
                  ("k_norm", 1), ("norm2", 8), ("b_gates", 2), ("lam_a", 2), ("lam_b", 2), ("cvec", 16),
                  ("b_ada", 48), ("norm_mix", 8), ("norm_mlp", 8), ("conv_w2", 36), ("conv_b2", 12), ("hyena_b", 4),
                  ("gla_norm", 1), ("gk_b", 4), ("filt_b", 3), ("filt_freq", 1)):
    COLS[_name] = (_n, _w)
    _n += _w
NCOLS = _n
CONST = {}
_n = 0
for _name, _w in (("ident", 128), ("ones", 128), ("causal_neg", 128), ("before", 128), ("group_m8", 32),
                  ("expert_m64", 32), ("expert", 32), ("lane_m8", 4), ("token", 4),
                  ("block_edge", 7), ("pair_edge", 8), ("extra", 18), ("steps", 32), ("eps", 1)):
    CONST[_name] = (_n, _w)
    _n += _w
NCONST = _n
NSTEP = 50
WS = {"gates": (0, 8), "router": (64, 36), "gk_low": (64 + 8 * 36, 32)}
NWS = 64 + 8 * 36 + 8 * 32


class Sem:

    def __init__(self, handle):
        self.h, self.n = handle, 0

    def up(self, ins):
        ins.then_inc(self.h, 1)
        self.n += 1
        return self.n


def mixer_moe_hyena(nc, x, w_in, w_out, w_gate, w_up, w_down, w_ada, ctx, w_in2, w_out2, w_mlp1, w_mlp2,
                    cols, consts, wsmall, bias36, dft, window, posz, filt_w, gk_w, consts2, norm_final, out):
    es = ExitStack()
    with es:
        def sb(name, shape, dt=F32):
            return es.enter_context(nc.sbuf_tensor(name, shape, dt))

        def sem(name):
            return Sem(es.enter_context(nc.semaphore(name)))

        PS = es.enter_context(nc.psum_tensor("PS", [P, 8, 512], F32))
        h_rows = nc.dram_tensor("h_rows", [T, D], F32, kind="Internal").ap()
        slot_token = nc.dram_tensor("slot_token", [SB_ * BS * NE, 1], I32, kind="Internal").ap()
        y_rows = nc.dram_tensor("y_rows", [2 * T + BS, D], F32, kind="Internal").ap()

        W = sb("W", [P, SLOTS, KD * CW])
        XN = sb("XN", [P, TT, D])
        HT = sb("HT", [P, KD, T])
        E1 = sb("E1", [P, 8, 512])
        VN = sb("VN", [P, TT, HEADS, HD + 1])
        MO = sb("MO", [P, TT, 512])
        QK = sb("QK", [P, 2 * HEADS, T])
        QT, KT = QK[:, 0:HEADS, :], QK[:, HEADS:, :]
        AV = sb("AV", [P, TT, 512])
        ROWS = sb("ROWS", [P, 4, T])
        TMP = sb("TMP", [P, 2, D])
        C = sb("C", [P, NCONST])
        V = sb("V", [P, NCOLS])
        WSM = sb("WSM", [P, NWS])
        ss = sb("ss", [P, TT, 8])
        rs = sb("rs", [P, TT, 8])
        gm = sb("gm", [P, 2, TT, HEADS])
        small = sb("small", [P, 8, 16])
        lam = sb("lam", [P, 4])
        MOD = sb("MOD", [P, 48, 2])
        SC = sb("SC", [P, 16])
        ints = TMP[:].rearrange("p a n -> p (a n)")
        IDX = ints[:, 0:SB_ * NE].bitcast(I32)
        STEP = ints[:, 256:256 + 2 * NSTEP + 2].bitcast(I32)
        XI = ints[:, 512:514].bitcast(I32)
        SI = ints[:, 514:516].bitcast(I32)
        GIDX = ints[:, 1024:1024 + SB_ * NE].bitcast(I32)

        def col(name, j=0, rows=P, base=0):
            s = COLS[name][0] + j
            return V[base:base + rows, s:s + 1]

        def colw(name):
            s, w = COLS[name]
            return V[:, s:s + w]

        def cst(name, rows=P):
            s, w = CONST[name]
            return C[0:rows, s:s + w]

        ident = cst("ident")
        ones = cst("ones")
        eps = cst("eps")

        x_in = [sem(f"x_in{t}") for t in range(TT)]
        const_in = sem("const_in")
        slot_in = [sem(f"slot_in{s}") for s in range(SLOTS)]
        vchain, achain = sem("vchain"), sem("achain")

        def done(eng, ins, s):
            eng.wait_ge(s.h, s.up(ins))

        def w_block(w, c0, width=CW):
            return w[:, c0:c0 + width].rearrange("(k p) c -> p k c", p=P)

        def slot(n):
            return W[:, n % SLOTS, :].rearrange("p (k c) -> p k c", c=CW)

        def flat(a):
            return a.rearrange("p m n -> p (m n)")

        def spread(a, n):
            return a.unsqueeze(2).to_broadcast([a.shape[0], a.shape[1], n])

        w1 = w_in[0]
        stream = [w_block(w1, 512 * j) for j in range(4)]
        stream += [w_block(w1, 2056 + 512 * j) for j in range(3)]
        stream += [w_block(w_ada[0], 512 * j) for j in range(12)]
        stream += [w_block(w_out[0], 0), w_block(w_out[0], 512)]
        N_PRE = len(stream)
        ADA0, OUT0 = 7, 19

        def arrived(eng, n):
            eng.wait_ge(slot_in[n % SLOTS].h, 16 * (n // SLOTS + 1))

        block = es.enter_context(nc.Block())

        @block.sync
        def _(sp):
            for t in range(TT):
                sp.dma_start(XN[:, t, :], x[0, t * P:(t + 1) * P, :]).then_inc(x_in[t].h, 16)
                if t == 0:
                    sp.dma_start(C[:], consts).then_inc(const_in.h, 16)
                    sp.dma_start(V[:], cols).then_inc(const_in.h, 16)
                    sp.dma_start(WSM[:], wsmall).then_inc(const_in.h, 16)

        def used(n):
            if n < ADA0:
                return proj, 4 * n + 4
            if n < OUT0:
                return ada_done, n - ADA0 + 1
            return wo_ready, 4 * (n - OUT0) + 4

        proj, ada_done, wo_ready = sem("proj"), sem("ada_done"), sem("wo_ready")

        @block.sync
        def _(sp):
            for n, src in enumerate(stream):
                if n >= SLOTS:
                    s, v = used(n - SLOTS)
                    sp.wait_ge(s.h, v)
                sp.dma_start(slot(n), src).then_inc(slot_in[n % SLOTS].h, 16)

        before_moe = [16 * len(range(s, N_PRE, SLOTS)) for s in range(SLOTS)]
        assert N_PRE % SLOTS == 3

        def expert_slots(s):
            return (3, 4, 5) if s == 0 else (0, 1, 2)

        def expert_chunks(e):
            if isinstance(e, int):
                g, u, d = w_gate[0, e], w_up[0, e], w_down[0, e]
            else:
                g, u, d = (w[0, bass.ds(e, 1)].rearrange("a r c -> (a r) c") for w in (w_gate, w_up, w_down))
            return (g.rearrange("(k p) c -> p k c", p=P), u.rearrange("(k p) c -> p k c", p=P),
                    d.rearrange("(k p) c -> p k c", p=P))

        def load_expert(sp, s, e, waits):
            for q, (n, src) in enumerate(zip(expert_slots(s), expert_chunks(e))):
                for w, v in waits[q]:
                    sp.wait_ge(w.h, v)
                dst = W[:, n, :].rearrange("p (k c) -> p k c", c=CW if q < 2 else D)
                sp.dma_start(dst, src).then_inc(slot_in[n].h, 16)

        @block.sync
        def _(sp):
            for s in range(2):
                load_expert(sp, s, s, [[used(N_PRE - SLOTS + 3 * s + q)] for q in range(3)])

        empty_set, table_emptied = sem("empty_set"), sem("table_emptied")

        @block.gpsimd
        def _(pool):
            empties = AV[0:BS, 0, 0:SB_ * NE].bitcast(I32)
            empty_set.up(pool.iota(empties, [[0, SB_ * NE]], base=2 * T, channel_multiplier=1))
            pool.wait_ge(empty_set.h, 1)
            pool.dma_start(slot_token.rearrange("(b s e) o -> s b (e o)", s=BS, e=NE),
                           empties.rearrange("s (b e) -> s b e", e=NE)).then_inc(table_emptied.h, 16)

        x_root, x_norm, x_turned, x_placed = sem("x_root"), sem("x_norm"), sem("x_turned"), sem("x_placed")

        def norm_and_turn(scale, dst, wait_rows, keep=None, shift=None, src=XN, tiles=TT, squares=None, stat0=0):
            root0, norm0, turned0, placed0 = x_root.n, x_norm.n, x_turned.n, x_placed.n

            def rows(t):
                return TMP[:, t % 2, :] if keep is None else keep[:, t, :]

            @block.scalar
            def _(act):
                for t in range(tiles):
                    wait_rows(act, t)
                    if t >= 2 and keep is None:
                        act.wait_ge(x_turned.h, turned0 + t - 1)
                    done(act, act.activation(rows(t) if squares is None else squares, src[:, t, :], ACT.Square,
                                         accum_out=ss[:, t + stat0, 0:1]), achain)
                    x_root.up(act.activation(rs[:, t + stat0, 0:1], ss[:, t + stat0, 0:1], ACT.Sqrt, bias=eps, scale=1.0 / D))

            @block.vector
            def _(dve):
                def place(t):
                    for b in range(2):
                        dve.wait_ge(x_turned.h, turned0 + t + 1)
                        o = dst[:, 4 * b:4 * b + 4, t * P:(t + 1) * P]
                        i = dve.tensor_tensor(o, PS[:, 4 + 2 * (t % 2) + b, :].rearrange("p (k n) -> p k n", k=4),
                                              spread(scale[:, 4 * b:4 * b + 4], P), ALU.mult)
                        if shift is not None:
                            done(dve, i, vchain)
                            i = dve.tensor_tensor(o, o, spread(shift[:, 4 * b:4 * b + 4], P), ALU.add)
                        x_placed.up(i)

                for t in range(tiles):
                    dve.wait_ge(x_root.h, root0 + t + 1)
                    done(dve, dve.reciprocal(rs[:, t + stat0, 1:2], rs[:, t + stat0, 0:1]), vchain)
                    x_norm.up(dve.tensor_scalar(rows(t), src[:, t, :], rs[:, t + stat0, 1:2], None, ALU.mult))
                    if t >= 1:
                        place(t - 1)
                place(tiles - 1)

            @block.tensor
            def _(pe):
                for t in range(tiles):
                    pe.wait_ge(x_norm.h, norm0 + t + 1)
                    if t >= 2:
                        pe.wait_ge(x_placed.h, placed0 + 2 * (t - 1))
                    for k in range(KD):
                        m = pe.transpose(PS[:, 4 + 2 * (t % 2) + k // 4, (k % 4) * P:(k % 4 + 1) * P],
                                         rows(t)[:, k * P:(k + 1) * P], ident)
                    x_turned.up(m)

        @block.scalar
        def _(act):
            act.wait_ge(const_in.h, 48)

        @block.vector
        def _(dve):
            dve.wait_ge(const_in.h, 48)

        @block.tensor
        def _(pe):
            pe.wait_ge(const_in.h, 48)

        norm_and_turn(colw("norm1"), HT, lambda eng, t: eng.wait_ge(x_in[t].h, 16))

        proj_act = sem("proj_act")
        gates_ready, gates_copied = sem("gates_ready"), sem("gates_copied")
        conv_done, silu_done, ones_set = sem("conv_done"), sem("silu_done"), sem("ones_set")
        qk_squared, qk_summed, qk_root, qk_normed = sem("qk_squared"), sem("qk_summed"), sem("qk_root"), sem("qk_normed")
        qk_turned, qk_placed = sem("qk_turned"), sem("qk_placed")
        groups = [("conv", j, "dve") for j in range(8)] + [("v", t, "act") for t in range(TT)]
        groups += [("o", t, "act") for t in range(TT)]
        groups += [("aq", t, "dve") for t in range(TT)] + [("ak", t, "dve") for t in range(TT)]
        groups += [("av", t, "act") for t in range(TT)]

        ADA_AT = {12: 0, 17: 1, 21: 2, 25: 3, 27: 4}
        ADA_DVE = 5
        ADA_SCALE = ((5, 6), (7, 8), (9, 10), (11,))
        ADA_HEAD = ((5,), (6, 7), (8, 9), (10, 11))

        def taken_before(g):
            kind = groups[g - 4][0]
            if kind == "conv":
                return conv_done, g - 3
            if kind in ("aq", "ak"):
                return qk_normed, g - 4 - 16 + 1
            return proj_act, sum(x[2] == "act" for x in groups[:g - 3])

        ada_summed, mod_done = sem("ada_summed"), sem("mod_done")
        CACC = TMP[:, 0, 512:1024]

        def ada_sum(dve, n):
            w = slot(ADA0 + n)
            arrived(dve, ADA0 + n)
            if n == 0:
                dve.wait_ge(silu_done.h, 1)
            if 0 < n < 4:
                dve.wait_ge(ada_done.h, n)
            sums = [(w[:, 0, :], 0)] if n >= 4 else [(CACC, 1), (w[:, 0, :], 0)]
            ready = [0, 0]
            for k in range(KD):
                for acc, v in sums:
                    c = SC[:, 2 * k + v:2 * k + v + 1]
                    if k == 0:
                        i = dve.tensor_scalar(acc, w[:, 0, :], c, None, ALU.mult)
                    else:
                        dve.wait_ge(vchain.h, ready[v])
                        i = dve.scalar_tensor_tensor(acc, w[:, k, :], c, acc, ALU.mult, ALU.add)
                    ready[v] = (vchain if k < KD - 1 else ada_summed).up(i)

        ada_scaled, ada_pooled = sem("ada_scaled"), sem("ada_pooled")

        def ada_scale(act, n):
            arrived(act, ADA0 + n)
            for k in range(KD):
                i = act.activation(slot(ADA0 + n)[:, k, :], slot(ADA0 + n)[:, k, :], ACT.Copy,
                                   scale=SC[:, 2 * k:2 * k + 1])
            ada_scaled.up(i)

        def ada_pool(pool, n):
            w = slot(ADA0 + n)
            pool.wait_ge(ada_scaled.h, n - ADA_DVE + 1)
            for half in (4, 2, 1):
                done(pool, pool.tensor_tensor(w[:, 0:half, :], w[:, 0:half, :], w[:, half:2 * half, :], ALU.add),
                     ada_pooled)

        def ada_turn(pe, n):
            if n == 0:
                pe.wait_ge(gates_copied.h, 2)
            if n < ADA_DVE:
                pe.wait_ge(ada_summed.h, 2 * n + 2 if n < 4 else n + 5)
            else:
                pe.wait_ge(ada_pooled.h, 3 * (n - ADA_DVE + 1))
            for c, acc in enumerate((slot(ADA0 + n)[:, 0, :], CACC)[:2 if n < 4 else 1]):
                for j in range(4):
                    m = pe.matmul(PS[:, 7, 8 * n + 2 * j + c:8 * n + 2 * j + c + 1], acc[:, j * P:(j + 1) * P],
                                  ones[:, 0:1], start=True, stop=True)
            ada_done.up(m)

        @block.tensor
        def _(pe):
            pe.wait_ge(x_placed.h, 2 * TT)

            def turn_qk(n):
                pe.wait_ge(qk_normed.h, n + 1)
                if n >= 2:
                    pe.wait_ge(qk_placed.h, n - 1)
                for h in range(HEADS):
                    m = pe.transpose(PS[:, 4 + n % 2, h * P:(h + 1) * P],
                                     TMP[:, 1, (n % 2) * 512 + h * P:(n % 2) * 512 + (h + 1) * P], ident)
                qk_turned.up(m)

            for g, (kind, j, who) in enumerate(groups):
                n = g // 4
                if g % 4 == 0:
                    arrived(pe, n)
                if g >= 4:
                    s, v = taken_before(g)
                    pe.wait_ge(s.h, v)
                for k in range(KD):
                    if kind == "conv":
                        m = pe.matmul(PS[:, g % 4, :], slot(n)[:, k, (g % 4) * P:(g % 4 + 1) * P], HT[:, k, :],
                                      start=k == 0, stop=k == KD - 1)
                    else:
                        m = pe.matmul(PS[:, g % 4, :], HT[:, k, j * P:(j + 1) * P], slot(n)[:, k, :],
                                      start=k == 0, stop=k == KD - 1)
                proj.up(m)
                if g == 7:
                    for q in range(2):
                        for k in range(KD):
                            m = pe.matmul(PS[0:4, 6 + q, :], WSM[:, 8 * k + 4 * q:8 * k + 4 * q + 4], HT[:, k, :],
                                          start=k == 0, stop=k == KD - 1)
                    gates_ready.up(m)
                if 18 <= g < 26:
                    turn_qk(g - 18)
                if g in ADA_AT:
                    ada_turn(pe, ADA_AT[g])

        @block.scalar
        def _(act):
            silu_done.up(act.activation(SC[:], colw("cvec"), ACT.Silu))
            for j in range(8):
                act.wait_ge(conv_done.h, j + 1)
                silu_done.up(act.activation(E1[:, j, :], E1[:, j, :], ACT.Silu))
            act.wait_ge(ones_set.h, 1)
            for g, (kind, j, who) in enumerate(groups):
                if kind == "conv":
                    continue
                act.wait_ge(proj.h, g + 1)
                bank = PS[:, g % 4, :]
                if kind == "v":
                    proj_act.up(act.activation(VN[:, j, :, 0:HD], bank.rearrange("p (h d) -> p h d", h=HEADS),
                                               ACT.Copy))
                elif kind == "o":
                    proj_act.up(act.activation(MO[:, j, :], bank, ACT.Sigmoid))
                elif kind == "av":
                    act.wait_ge(table_emptied.h, 16)
                    proj_act.up(act.activation(AV[:, j, :], bank, ACT.Copy))
                else:
                    n = g - 16
                    act.wait_ge(qk_summed.h, n) if n else None
                    qk_squared.up(act.activation(TMP[:, 0, 0:512], bank, ACT.Square))
                    act.wait_ge(qk_summed.h, n + 1)
                    qk_root.up(act.activation(rs[:, n % 4, :], ss[:, n % 4, :], ACT.Sqrt, bias=eps, scale=1.0 / 64))

        @block.vector
        def _(dve):
            ones_set.up(dve.memset(VN[:, :, :, HD:HD + 1], 1.0))
            done(dve, dve.tensor_tensor(lam[:, 2:3], col("q_norm"), col("k_norm"), ALU.mult), vchain)
            done(dve, dve.tensor_scalar(lam[:, 2:3], lam[:, 2:3], 64 ** -0.5, None, ALU.mult), vchain)
            for j in range(8):
                dve.wait_ge(proj.h, j + 1)
                bank = PS[:, j % 4, :]
                done(dve, dve.tensor_scalar(E1[:, j, :], bank, col("conv_w", 24 + j), col("conv_b", j),
                                            ALU.mult, ALU.add), vchain)
                for s in (1, 2, 3):
                    i = dve.scalar_tensor_tensor(E1[:, j, s:], bank[:, 0:T - s], col("conv_w", 8 * (3 - s) + j),
                                                 E1[:, j, s:], ALU.mult, ALU.add)
                    if s < 3:
                        done(dve, i, vchain)
                done(dve, i, conv_done)
            dve.wait_ge(gates_ready.h, 1)
            for q in range(2):
                gates_copied.up(dve.tensor_scalar(ROWS[0:4, q, :], PS[0:4, 6 + q, :], col("b_gates", q, 4), None,
                                                  ALU.add))
            ada_sum(dve, 0)
            ada_sum(dve, 1)
            for n in range(8):
                g = 16 + n
                dve.wait_ge(qk_squared.h, n + 1)
                done(dve, dve.tensor_reduce(ss[:, n % 4, :], TMP[:, 0, 0:512].rearrange("p (g d) -> p g d", g=8),
                                            AX.X, ALU.add), qk_summed)
                dve.wait_ge(qk_root.h, n + 1)
                done(dve, dve.reciprocal(rs[:, n % 4, :], rs[:, n % 4, :]), vchain)
                if n >= 2:
                    dve.wait_ge(qk_turned.h, n - 1)
                done(dve, dve.tensor_tensor(
                    TMP[:, 1, (n % 2) * 512:(n % 2 + 1) * 512].rearrange("p (g d) -> p g d", g=8),
                    PS[:, g % 4, :].rearrange("p (g d) -> p g d", g=8), spread(rs[:, n % 4, :], 64), ALU.mult),
                    qk_normed)

                def place_qk(m):
                    dve.wait_ge(qk_turned.h, m + 1)
                    src = PS[:, 4 + m % 2, :].rearrange("p (h n) -> p h n", h=HEADS)
                    t = m % 4
                    if m < 4:
                        i = dve.tensor_scalar(QT[:, :, t * P:(t + 1) * P], src, lam[:, 2:3], None, ALU.mult)
                    else:
                        i = dve.tensor_copy(KT[:, :, t * P:(t + 1) * P], src)
                    qk_placed.up(i)
                if n >= 2:
                    place_qk(n - 2)
                if n in (2, 5):
                    ada_sum(dve, 2 if n == 2 else 3)
            place_qk(6)
            place_qk(7)
            ada_sum(dve, 4)

        gate_ln, rows_ready, gates_turned, gate_cols, m_exp = (
            sem("gate_ln"), sem("rows_ready"), sem("gates_turned"), sem("gate_cols"), sem("m_exp"))
        lam_in, lam_sum, lam_exp = sem("lam_in"), sem("lam_sum"), sem("lam_exp")
        one, fgate, tmpr, neg_g = (ROWS[0:4, q, :] for q in range(4))

        @block.scalar
        def _(act):
            act.wait_ge(gates_copied.h, 2)
            done(act, act.activation(tmpr, fgate, ACT.Abs), achain)
            done(act, act.activation(tmpr, tmpr, ACT.Exp, scale=-1.0), achain)
            gate_ln.up(act.activation(tmpr, tmpr, ACT.Ln, bias=1.0))

        @block.vector
        def _(dve):
            lam_in.up(dve.tensor_tensor(lam[:, 0:2], colw("lam_a"), colw("lam_b"), ALU.mult))
            dve.memset(neg_g, 1.0).then_inc(vchain.h, 1)
            vchain.n += 1
            dve.wait_ge(gate_ln.h, 1)
            done(dve, dve.scalar_tensor_tensor(fgate, fgate, 0.0, tmpr, ALU.min, ALU.subtract), vchain)
            done(dve, dve.tensor_tensor_scan(tmpr, neg_g, fgate, 0.0, ALU.mult, ALU.add), vchain)
            done(dve, dve.tensor_tensor(one, one, tmpr, ALU.subtract), vchain)
            done(dve, dve.tensor_tensor_scan(fgate, one, one, 0.0, ALU.max, ALU.max), vchain)
            done(dve, dve.tensor_tensor(tmpr, tmpr, fgate, ALU.add), vchain)
            rows_ready.up(dve.tensor_scalar(neg_g, fgate, -1.0, None, ALU.mult))

        @block.tensor
        def _(pe):
            pe.wait_ge(rows_ready.h, 1)
            for q, r in enumerate((one, tmpr)):
                for t in range(TT):
                    pe.transpose(PS[:, 6, 16 * q + 4 * t:16 * q + 4 * t + 4], r[:, t * P:(t + 1) * P], ident[0:4, 0:4])
            pe.wait_ge(lam_in.h, 1)
            gates_turned.up(pe.matmul(PS[:, 6, 64:66], ones, lam[:, 0:2], start=True, stop=True))

        @block.vector
        def _(dve):
            dve.wait_ge(gates_turned.h, 1)
            gate_cols.up(dve.tensor_copy(gm[:, 0], PS[:, 6, 0:16].rearrange("p (t h) -> p t h", t=TT)))

        @block.scalar
        def _(act):
            act.wait_ge(gates_turned.h, 1)
            act.wait_ge(gate_cols.h, 1)
            m_exp.up(act.activation(gm[:, 1], PS[:, 6, 16:32].rearrange("p (t h) -> p t h", t=TT), ACT.Exp,
                                    scale=-1.0))
            lam_exp.up(act.activation(lam[:, 0:2], PS[:, 6, 64:66], ACT.Exp))

        @block.vector
        def _(dve):
            dve.wait_ge(lam_exp.h, 1)
            done(dve, dve.tensor_tensor(lam[:, 3:4], lam[:, 1:2], lam[:, 0:1], ALU.subtract), vchain)
            done(dve, dve.tensor_scalar(lam[:, 3:4], lam[:, 3:4], -LAMBDA_INIT, None, ALU.add), vchain)

        HTf = HT[:].rearrange("p k n -> p (k n)")
        OFF = [0, 512, 896, 1152]

        def decay(h, s):
            o = (h % 2) * 1280 + OFF[s]
            return HTf[:, o:o + T - s * P]

        ARG = HTf[:, 2560:3584].rearrange("p (b s n) -> p b s n", b=2, s=TT)
        score_bank = [(2, 0), (3, 0), (4, 0), (4, 256)]
        g_spread, decay_arg, decay_done = sem("g_spread"), sem("decay_arg"), sem("decay_done")
        scores, weighted, num_ready, hm_done = sem("scores"), sem("weighted"), sem("num_ready"), sem("hm_done")

        @block.tensor
        def _(pe):
            pe.wait_ge(proj_act.h, 12)
            pe.wait_ge(silu_done.h, 9)
            pe.wait_ge(qk_placed.h, 8)
            pe.wait_ge(m_exp.h, 1)
            pe.wait_ge(lam_exp.h, 1)

            def spread_g(h):
                if h >= 2:
                    pe.wait_ge(decay_done.h, 7 * (h - 1))
                pick = ident[0:4, h:h + 1].to_broadcast([4, P])
                g_spread.up(pe.matmul(PS[:, h % 2, :], pick, neg_g, start=True, stop=True))

            def score(h):
                if h:
                    pe.wait_ge(weighted.h, 4 * h)
                for s in range(TT):
                    b, o = score_bank[s]
                    m = pe.matmul(PS[:, b, o:o + T - s * P], E1[:, 4 + h, s * P:(s + 1) * P], E1[:, h, s * P:],
                                  start=True, stop=True)
                scores.up(m)

            def values(h):
                pe.wait_ge(weighted.h, 4 * h + 4)
                if h:
                    pe.wait_ge(hm_done.h, 4 * h)
                for t in range(TT):
                    for s in range(t + 1):
                        m = pe.matmul(PS[:, 5 + t // 2, (t % 2) * (HD + 1):(t % 2 + 1) * (HD + 1)],
                                      decay(h, s)[:, (t - s) * P:(t - s + 1) * P], VN[:, s, h, :],
                                      start=s == 0, stop=s == t)
                num_ready.up(m)

            spread_g(0)
            score(0)
            for h in range(HEADS):
                if h + 1 < HEADS:
                    spread_g(h + 1)
                    score(h + 1)
                values(h)
                for n in ADA_HEAD[h]:
                    ada_turn(pe, n)

        @block.scalar
        def _(act):
            act.wait_ge(gate_cols.h, 1)
            for h in range(HEADS):
                act.wait_ge(g_spread.h, h + 1)
                if h >= 2:
                    act.wait_ge(num_ready.h, h - 1)
                act.wait_ge(decay_arg.h, 4 * h + 4)
                for s in range(TT - 1):
                    decay_done.up(act.activation(decay(h, s)[:, P:], PS[:, h % 2, (s + 1) * P:T], ACT.Exp,
                                                 bias=gm[:, 0, s, h:h + 1]))
                for s in range(TT):
                    decay_done.up(act.activation(decay(h, s)[:, 0:P], ARG[:, h % 2, s, :], ACT.Exp))
                for n in ADA_SCALE[h]:
                    ada_scale(act, n)

        @block.gpsimd
        def _(pool):
            for n in range(ADA_DVE, 12):
                ada_pool(pool, n)

        @block.vector
        def _(dve):
            dve.wait_ge(gate_cols.h, 1)

            def args(h):
                dve.wait_ge(g_spread.h, h + 1)
                if h >= 2:
                    dve.wait_ge(decay_done.h, 7 * (h - 1))
                for s in range(TT):
                    decay_arg.up(dve.scalar_tensor_tensor(ARG[:, h % 2, s, :], PS[:, h % 2, s * P:(s + 1) * P],
                                                          gm[:, 0, s, h:h + 1], cst("causal_neg"), ALU.add, ALU.add))

            args(0)
            dve.wait_ge(m_exp.h, 1)
            for h in range(HEADS):
                if h + 1 < HEADS:
                    args(h + 1)
                dve.wait_ge(scores.h, h + 1)
                dve.wait_ge(decay_done.h, 7 * h + 7)
                for s in range(TT):
                    b, o = score_bank[s]
                    weighted.up(dve.scalar_tensor_tensor(decay(h, s), PS[:, b, o:o + T - s * P], HD ** -0.5,
                                                         decay(h, s), ALU.mult, ALU.mult))
                dve.wait_ge(num_ready.h, h + 1)
                nd = PS[:, 5:7, 0:2 * (HD + 1)].rearrange("p b (t n) -> p b t n", t=2)
                den, ab = small[:, 0, 0:4], small[:, 1, 0:4]
                for b in range(2):
                    done(dve, dve.tensor_copy(den[:, 2 * b:2 * b + 2], nd[:, b, :, HD]), vchain)
                done(dve, dve.scalar_tensor_tensor(ab, den, -1.0, den, ALU.mult, ALU.max), vchain)
                done(dve, dve.tensor_tensor(ab, ab, gm[:, 1, :, h], ALU.max), vchain)
                done(dve, dve.reciprocal(ab, ab), vchain)
                for t in range(TT):
                    o = MO[:, t, h * HD:(h + 1) * HD]
                    hm_done.up(dve.scalar_tensor_tensor(o, nd[:, t // 2, t % 2, 0:HD], ab[:, t:t + 1], o,
                                                        ALU.mult, ALU.mult))
            dve.wait_ge(ada_done.h, 12)
            mod = PS[:, 7, 0:96].rearrange("p (j c) -> p j c", c=2)
            for c, w in enumerate((48, 16)):
                mod_done.up(dve.tensor_tensor(MOD[:, 0:w, c], mod[:, 0:w, c], colw("b_ada")[:, 0:w], ALU.add))
            dve.wait_ge(mod_done.h, 2)

        head_sum, head_root, head_normed, head_turned, head_placed = (
            sem("head_sum"), sem("head_root"), sem("head_normed"), sem("head_turned"), sem("head_placed"))

        def head_norm(src, norm_col, dst, factor, sq=TMP[:].rearrange("p a n -> p (a n)"), gate=None):
            i = head_root.n

            @block.vector
            def _(dve):
                done(dve, dve.tensor_tensor(sq, flat(src), flat(src), ALU.mult), vchain)
                head_sum.up(dve.tensor_reduce(small[:, 2, :], sq.rearrange("p (g d) -> p g d", d=HD), AX.X, ALU.add))

            @block.scalar
            def _(act):
                act.wait_ge(head_sum.h, head_sum.n)
                head_root.up(act.activation(small[:, 3, :], small[:, 2, :], ACT.Sqrt, bias=eps, scale=1.0 / HD))

            @block.vector
            def _(dve):
                dve.wait_ge(head_root.h, i + 1)
                done(dve, dve.reciprocal(small[:, 3, :], small[:, 3, :]), vchain)
                if factor != 1.0:
                    done(dve, dve.tensor_scalar(small[:, 3, :], small[:, 3, :], factor, None, ALU.mult), vchain)
                for t in range(TT):
                    v = src[:, t, :].rearrange("p (h d) -> p h d", h=HEADS)
                    head_normed.up(dve.tensor_tensor(v, v, spread(small[:, 3, 4 * t:4 * t + 4], HD), ALU.mult))

            @block.tensor
            def _(pe):
                for t in range(TT):
                    pe.wait_ge(head_normed.h, 4 * i + t + 1)
                    if t >= 2:
                        pe.wait_ge(head_placed.h, 4 * i + t - 1)
                    for h in range(HEADS):
                        m = pe.transpose(PS[:, 4 + t % 2, h * P:(h + 1) * P], src[:, t, h * P:(h + 1) * P], ident)
                    head_turned.up(m)

            @block.vector
            def _(dve):
                for t in range(TT):
                    dve.wait_ge(head_turned.h, 4 * i + t + 1)
                    o = dst[:, :, t * P:(t + 1) * P]
                    p = PS[:, 4 + t % 2, :].rearrange("p (h n) -> p h n", h=HEADS)
                    if gate is None:
                        head_placed.up(dve.tensor_scalar(o, p, col(norm_col), None, ALU.mult))
                    else:
                        head_placed.up(dve.scalar_tensor_tensor(o, p, col(norm_col), gate[:, :, t * P:(t + 1) * P],
                                                                ALU.mult, ALU.mult))

        @block.vector
        def _(dve):
            dve.wait_ge(hm_done.h, 16)
            dve.wait_ge(num_ready.h, 4)
            dve.wait_ge(qk_turned.h, 8)

        PB = VN[:].rearrange("p t h d -> p (t h d)")[:, 0:2048].rearrange("p (b n) -> p b n", b=4)
        AT = E1[:, 4:6, :]
        HA = E1[:, 0:4, :]
        neg_max, exp_done, mixed = sem("neg_max"), sem("exp_done"), sem("mixed")
        a_scores, a_turned, a_placed, a_out, a_kept = (
            sem("a_scores"), sem("a_turned"), sem("a_placed"), sem("a_out"), sem("a_kept"))
        units = [(h, q) for h in range(HEADS) for q in range(TT)]
        SUMS, ROOT = (small[:, 2, :], small[:, 7, :]), (small[:, 3, :], small[:, 1, :])
        NM, SM, RD = small[:, 4, :], small[:, 5, :], small[:, 6, :]

        @block.tensor
        def _(pe):
            pe.wait_ge(decay_done.h, 28)
            pe.wait_ge(weighted.h, 16)
            pe.wait_ge(hm_done.h, 16)
            pe.wait_ge(mod_done.h, 2)

            def score(v):
                h, q = units[v]
                n = (q + 1) * P
                if v >= 2:
                    pe.wait_ge(exp_done.h, 2 * (v - 1))
                for c in range(2):
                    m = pe.matmul(PS[:, (2 * v + c) % 4, 0:n], QT[64 * c:64 * c + 64, h, q * P:(q + 1) * P],
                                  KT[64 * c:64 * c + 64, h, 0:n], start=True, stop=True)
                    a_scores.up(m)

            def times_values(v):
                h, q = units[v]
                pe.wait_ge(a_placed.h, v + 1)
                if v >= 2:
                    pe.wait_ge(a_kept.h, v - 1)
                for s in range(q + 1):
                    m = pe.matmul(PS[:, 6 + v % 2, 0:HD], AT[:, v % 2, s * P:(s + 1) * P],
                                  AV[:, s, h * HD:(h + 1) * HD], start=s == 0, stop=s == q)
                a_out.up(m)

            score(0)
            score(1)
            for v, (h, q) in enumerate(units):
                if v + 2 < len(units):
                    score(v + 2)
                pe.wait_ge(mixed.h, v + 1)
                if v >= 2:
                    pe.wait_ge(a_placed.h, v - 1)
                for s in range(q + 1):
                    m = pe.transpose(PS[:, 4 + v % 2, s * P:(s + 1) * P],
                                     PB[:, (2 * v) % 4, s * P:(s + 1) * P], ident)
                a_turned.up(m)
                if v:
                    times_values(v - 1)
            times_values(len(units) - 1)

        @block.scalar
        def _(act):
            def place(v):
                n = (units[v][1] + 1) * P
                act.wait_ge(a_turned.h, v + 1)
                if v >= 2:
                    act.wait_ge(a_out.h, v - 1)
                a_placed.up(act.activation(AT[:, v % 2, 0:n], PS[:, 4 + v % 2, 0:n], ACT.Copy))

            def square(src, t, h, a):
                done(act, act.activation(TMP[:, 0, 0:HD], src[:, t, h * HD:(h + 1) * HD], ACT.Square,
                                         accum_out=SUMS[a][:, 4 * t + h:4 * t + h + 1]), achain)

            act.wait_ge(hm_done.h, 16)
            for v, (h, q) in enumerate(units):
                n = (q + 1) * P
                for c in range(2):
                    u = 2 * v + c
                    act.wait_ge(neg_max.h, u + 1)
                    if v >= 2:
                        act.wait_ge(a_turned.h, v - 1)
                    exp_done.up(act.activation(PB[:, u % 4, 0:n], PS[:, u % 4, 0:n], ACT.Exp,
                                               bias=NM[:, u % 4:u % 4 + 1], accum_out=SM[:, u % 4:u % 4 + 1]))
                if v >= 1:
                    place(v - 1)
                square(MO, v // 4, v % 4, 0)
                if v >= 3:
                    act.wait_ge(a_kept.h, v - 2)
                    square(HA, units[v - 3][1], units[v - 3][0], 1)
            place(len(units) - 1)
            for v in range(len(units) - 3, len(units)):
                act.wait_ge(a_kept.h, v + 1)
                square(HA, units[v][1], units[v][0], 1)
            for a in range(2):
                head_root.up(act.activation(ROOT[a], SUMS[a], ACT.Sqrt, bias=eps, scale=1.0 / HD))

        @block.vector
        def _(dve):
            def maxima(v):
                h, q = units[v]
                n = (q + 1) * P
                for c in range(2):
                    u = 2 * v + c
                    dve.wait_ge(a_scores.h, u + 1)
                    done(dve, dve.memset(PS[0:64, u % 4, n - 64:n], -BIG), vchain)
                    if u >= 4:
                        dve.wait_ge(exp_done.h, u - 3)
                    neg_max.up(dve.tensor_reduce(NM[:, u % 4:u % 4 + 1], PS[:, u % 4, 0:n], AX.X, ALU.max,
                                                 negate=True))

            def keep(v):
                h, q = units[v]
                dve.wait_ge(a_out.h, v + 1)
                a_kept.up(dve.tensor_copy(HA[:, q, h * HD:(h + 1) * HD], PS[:, 6 + v % 2, 0:HD]))

            maxima(0)
            maxima(1)
            for v, (h, q) in enumerate(units):
                n = (q + 1) * P
                a, b = (2 * v) % 4, (2 * v + 1) % 4
                dve.wait_ge(exp_done.h, 2 * v + 2)
                done(dve, dve.reciprocal(RD[:, a:b + 1], SM[:, a:b + 1]), vchain)
                done(dve, dve.tensor_scalar(PB[:, b, 0:n], PB[:, b, 0:n], RD[:, b:b + 1], lam[:, 3:4],
                                            ALU.mult, ALU.mult), vchain)
                mixed.up(dve.scalar_tensor_tensor(PB[:, a, 0:n], PB[:, a, 0:n], RD[:, a:a + 1], PB[:, b, 0:n],
                                                  ALU.mult, ALU.add))
                if v + 2 < len(units):
                    maxima(v + 2)
                if v >= 2:
                    keep(v - 2)
            keep(len(units) - 2)
            keep(len(units) - 1)
            dve.wait_ge(a_kept.h, len(units))

        @block.vector
        def _(dve):
            def place(u):
                a, t = divmod(u, 4)
                dve.wait_ge(head_turned.h, u + 1)
                head_placed.up(dve.tensor_scalar(HT[:, 4 * a:4 * a + 4, t * P:(t + 1) * P],
                                                 PS[:, 4 + u % 2, :].rearrange("p (h n) -> p h n", h=HEADS),
                                                 col(("m_norm", "a_norm")[a]), None, ALU.mult))

            for u in range(8):
                a, t = divmod(u, 4)
                if t == 0:
                    dve.wait_ge(head_root.h, a + 1)
                    done(dve, dve.reciprocal(ROOT[a], ROOT[a]), vchain)
                    if a:
                        done(dve, dve.tensor_scalar(ROOT[a], ROOT[a], 1.0 - LAMBDA_INIT, None, ALU.mult), vchain)
                v = (MO, HA)[a][:, t, :].rearrange("p (h d) -> p h d", h=HEADS)
                head_normed.up(dve.tensor_tensor(v, v, spread(ROOT[a][:, 4 * t:4 * t + 4], HD), ALU.mult))
                if u >= 2:
                    place(u - 2)
            place(6)
            place(7)

        @block.tensor
        def _(pe):
            for u in range(8):
                a, t = divmod(u, 4)
                pe.wait_ge(head_normed.h, u + 1)
                if u >= 2:
                    pe.wait_ge(head_placed.h, u - 1)
                for h in range(HEADS):
                    m = pe.transpose(PS[:, 4 + u % 2, h * P:(h + 1) * P], (MO, HA)[a][:, t, h * P:(h + 1) * P], ident)
                head_turned.up(m)

        x1_done = sem("x1_done")

        @block.tensor
        def _(pe):
            pe.wait_ge(head_placed.h, 8)
            pe.wait_ge(exp_done.h, 32)
            for c in range(2):
                arrived(pe, OUT0 + c)
                for t in range(TT):
                    g = 4 * c + t
                    if g >= 4:
                        pe.wait_ge(x1_done.h, g - 3)
                    for k in range(KD):
                        m = pe.matmul(PS[:, g % 4, :], HT[:, k, t * P:(t + 1) * P], slot(OUT0 + c)[:, k, :],
                                      start=k == 0, stop=k == KD - 1)
                    wo_ready.up(m)

        @block.vector
        def _(dve):
            for g in range(8):
                c, t = divmod(g, 4)
                dve.wait_ge(wo_ready.h, g + 1)
                xr = XN[:, t, c * 512:(c + 1) * 512]
                x1_done.up(dve.tensor_tensor(xr, xr, PS[:, g % 4, :], ALU.add))

        h_out, logits_ready, bias_in = sem("h_out"), sem("logits_ready"), sem("bias_in")
        RV = AV[:].rearrange("p t n -> p (t n)")
        HR = QK[:].rearrange("p (t a) n -> p t (a n)", a=2)
        taken = [0]

        def scratch(*dims):
            n = int(np.prod(dims))
            a = RV[:, taken[0]:taken[0] + n]
            taken[0] += n
            if len(dims) == 2:
                a = a.rearrange("p (a b) -> p a b", b=dims[1])
            return a

        rbias = scratch(NG + NE)

        @block.gpsimd
        def _(pool):
            pool.wait_ge(a_out.h, 16)
            pool.dma_start(rbias, bias36.to_broadcast([P, NG + NE])).then_inc(bias_in.h, 16)

        @block.vector
        def _(dve):
            dve.wait_ge(head_turned.h, 8)
            dve.wait_ge(x1_done.h, 8)

        norm_and_turn(colw("norm2"), E1, lambda eng, t: eng.wait_ge(x1_done.h, 5 + t), keep=HR)

        @block.sync
        def _(sp):
            for t in range(TT):
                sp.wait_ge(x_norm.h, 4 + t + 1)
                sp.dma_start(h_rows[t * P:(t + 1) * P, :], HR[:, t, :]).then_inc(h_out.h, 16)

        @block.tensor
        def _(pe):
            for t in range(TT):
                pe.wait_ge(x_placed.h, 2 * TT + 2 * t + 2)
                for k in range(KD):
                    r0 = WS["router"][0] + 36 * k
                    m = pe.matmul(PS[:, 0, 36 * t:36 * t + 36], E1[:, k, t * P:(t + 1) * P], WSM[:, r0:r0 + 36],
                                  start=k == 0, stop=k == KD - 1)
            logits_ready.up(m)

        lg = scratch(TT, 36)
        gd, ge, eq4 = scratch(TT, NG), scratch(TT, NG), scratch(TT, NG)
        gmax, gsum, gw, gi, m1, m2, i1, i2, e2, wden = (scratch(TT) for _ in range(10))
        mask, ml, t32, oh1, oh2, both, v1 = (scratch(TT, NE) for _ in range(7))
        wk = ss[:].rearrange("p t g -> p (t g)")[:, 0:2 * TT].rearrange("p (q t) -> p q t", q=2)
        destf = scratch(2, TT)
        cnt, nblk, cum = scratch(NE), scratch(NE), scratch(NE)
        rowf = ROWS[:].rearrange("p q n -> p (q n)")
        cmp7 = rowf[:, 0:NE * 7].rearrange("p (a b) -> p a b", b=7)
        le, t18 = (rowf[:, o:o + 18 * NE].rearrange("p (a b) -> p a b", b=NE) for o in (256, 896))
        ej, bj = scratch(18), scratch(18)
        npair = scratch(10)
        stepf = scratch(2, NSTEP)
        assert taken[0] <= 2048
        DEST = rs[:].rearrange("p t g -> p (t g)")[:, 0:8].bitcast(I32).rearrange("p (q t) -> p q t", q=2)
        TOK = rs[:].rearrange("p t g -> p (t g)")[:, 16:24].bitcast(I32).rearrange("p (q t) -> p q t", q=2)
        exp_in, exp_out, choice_ready, ranks_ready, dest_ready, step_ready = (
            sem("exp_in"), sem("exp_out"), sem("choice_ready"), sem("ranks_ready"), sem("dest_ready"),
            sem("step_ready"))
        rows_known = sem("rows_known")
        scattered = sem("scattered")
        y_out = [sem("y_out0"), sem("y_out1")]

        def per_t(a, n):
            return a.unsqueeze(1).to_broadcast([P, TT, n])

        @block.vector
        def _(dve):
            def op(ins):
                done(dve, ins, vchain)

            dve.wait_ge(logits_ready.h, 1)
            dve.wait_ge(bias_in.h, 16)
            op(dve.tensor_tensor(lg, PS[:, 0, 0:144].rearrange("p (t n) -> p t n", t=TT), per_t(rbias, 36), ALU.add))
            op(dve.tensor_reduce(gmax, lg[:, :, 0:NG], AX.X, ALU.max))
            done(dve, dve.tensor_tensor(gd, lg[:, :, 0:NG], spread(gmax, NG), ALU.subtract), exp_in)
            op(dve.tensor_scalar(eq4, gd, 0.0, None, ALU.is_equal))
            op(dve.tensor_tensor(eq4, eq4, per_t(cst("lane_m8"), NG), ALU.mult))
            op(dve.tensor_reduce(gi, eq4, AX.X, ALU.min))
            op(dve.tensor_tensor(mask, per_t(cst("group_m8"), NE), spread(gi, NE), ALU.is_equal))
            op(dve.tensor_tensor(ml, lg[:, :, NG:], mask, ALU.mult))
            op(dve.tensor_scalar(mask, mask, BIG, -BIG, ALU.mult, ALU.add))
            op(dve.tensor_tensor(ml, ml, mask, ALU.add))

            def first_max(mx, ix, oh):
                op(dve.tensor_reduce(mx, ml, AX.X, ALU.max))
                op(dve.tensor_tensor(t32, ml, spread(mx, NE), ALU.is_equal))
                op(dve.tensor_tensor(t32, t32, per_t(cst("expert_m64"), NE), ALU.mult))
                op(dve.tensor_reduce(ix, t32, AX.X, ALU.min))
                op(dve.tensor_tensor(oh, per_t(cst("expert_m64"), NE), spread(ix, NE), ALU.is_equal))

            first_max(m1, i1, oh1)
            op(dve.tensor_scalar(t32, oh1, -2.0 * BIG, None, ALU.mult))
            op(dve.tensor_tensor(ml, ml, t32, ALU.add))
            first_max(m2, i2, oh2)
            done(dve, dve.tensor_tensor(both, oh1, oh2, ALU.add), choice_ready)
            done(dve, dve.tensor_tensor(e2, m2, m1, ALU.subtract), exp_in)
            dve.wait_ge(exp_out.h, 2)
            op(dve.tensor_reduce(gsum, ge, AX.X, ALU.add))
            op(dve.tensor_scalar(wden, e2, 1.0, None, ALU.add))
            op(dve.tensor_tensor(wden, wden, gsum, ALU.mult))
            op(dve.reciprocal(wk[:, 0, :], wden))
            op(dve.tensor_tensor(wk[:, 1, :], wk[:, 0, :], e2, ALU.mult))
            dve.wait_ge(ranks_ready.h, 1)
            rank = PS[:, 1, 0:128].rearrange("p (t e) -> p t e", t=TT)
            op(dve.tensor_scalar(v1, rank, float(NE), None, ALU.mult))
            op(dve.tensor_tensor(v1, v1, per_t(cst("expert"), NE), ALU.add))
            for q, oh in enumerate((oh1, oh2)):
                op(dve.tensor_tensor(t32, v1, oh, ALU.mult))
                op(dve.tensor_reduce(destf[:, q, :], t32, AX.X, ALU.add))
                op(dve.tensor_scalar(TOK[:, q, :], cst("token"), float(q * T), None, ALU.add))
            done(dve, dve.tensor_copy(DEST, destf), dest_ready)
            one_row = lambda a: a[0:1]
            op(dve.tensor_copy(one_row(cnt), PS[0:1, 2, 0:NE]))
            op(dve.tensor_tensor(one_row(cmp7), one_row(cnt).unsqueeze(2).to_broadcast([1, NE, 7]),
                                 cst("block_edge", 1).unsqueeze(1).to_broadcast([1, NE, 7]), ALU.is_gt))
            op(dve.tensor_reduce(one_row(nblk), one_row(cmp7), AX.X, ALU.add))
            op(dve.tensor_tensor_scan(one_row(cum), cst("ones", 1)[:, 0:NE], one_row(nblk), 0.0, ALU.mult, ALU.add))
            op(dve.tensor_tensor(one_row(le), one_row(cum).unsqueeze(1).to_broadcast([1, 18, NE]),
                                 cst("extra", 1).unsqueeze(2).to_broadcast([1, 18, NE]), ALU.is_le))
            op(dve.tensor_reduce(one_row(ej), one_row(le), AX.X, ALU.add))
            op(dve.tensor_tensor(one_row(t18), one_row(le), one_row(nblk).unsqueeze(1).to_broadcast([1, 18, NE]),
                                 ALU.mult))
            op(dve.tensor_reduce(one_row(bj), one_row(t18), AX.X, ALU.add))
            op(dve.tensor_tensor(one_row(bj), cst("extra", 1), one_row(bj), ALU.subtract))
            op(dve.tensor_scalar(one_row(bj), one_row(bj), 1.0, SB_ - 1.0, ALU.add, ALU.min))
            for q in range(2):
                op(dve.tensor_copy(stepf[0:1, q, 0:NE], cst("expert", 1)))
            op(dve.tensor_scalar(stepf[0:1, 0, NE:], one_row(ej), NE - 1.0, None, ALU.min))
            op(dve.scalar_tensor_tensor(stepf[0:1, 1, NE:], one_row(bj), float(NE), stepf[0:1, 0, NE:],
                                        ALU.mult, ALU.add))
            op(dve.tensor_scalar(npair[0:1, 0:8], cst("pair_edge", 1), cum[0:1, NE - 1:NE], None, ALU.is_lt))
            op(dve.tensor_reduce(npair[0:1, 8:9], npair[0:1, 0:8], AX.X, ALU.add))
            op(dve.tensor_scalar(npair[0:1, 8:9], npair[0:1, 8:9], 1.0, 16.0, ALU.max, ALU.add))
            op(dve.tensor_scalar(npair[0:1, 9:10], npair[0:1, 8:9], -1.0, None, ALU.add))
            op(dve.tensor_copy(STEP[0:1, 2 * NSTEP:], npair[0:1, 8:10]))
            done(dve, dve.tensor_copy(STEP[0:1, 0:2 * NSTEP],
                                      stepf[0:1].rearrange("p a b -> p (a b)")), step_ready)

        @block.scalar
        def _(act):
            act.wait_ge(exp_in.h, 1)
            exp_out.up(act.activation(ge, gd, ACT.Exp))
            act.wait_ge(exp_in.h, 2)
            exp_out.up(act.activation(e2, e2, ACT.Exp))

        @block.tensor
        def _(pe):
            pe.wait_ge(choice_ready.h, 1)
            for t in range(TT):
                pe.matmul(PS[:, 1, NE * t:NE * (t + 1)], cst("before"), both[:, t, :], start=True, stop=t == 0)
                for j in range(t):
                    m = pe.matmul(PS[:, 1, NE * t:NE * (t + 1)], ones, both[:, j, :], start=False, stop=j == t - 1)
            for t in range(TT):
                m = pe.matmul(PS[:, 2, 0:NE], ones, both[:, t, :], start=t == 0, stop=t == TT - 1)
            ranks_ready.up(m)

        @block.gpsimd
        def _(pool):
            pool.wait_ge(dest_ready.h, 1)
            pool.wait_ge(table_emptied.h, 16)
            for q in range(2):
                for t in range(TT):
                    pool.indirect_dma_start(slot_token, bass.IndirectOffsetOnAxis(ap=DEST[:, q, t:t + 1], axis=0),
                                            TOK[:, q, t:t + 1], None).then_inc(scattered.h, 16)
            pool.wait_ge(scattered.h, 16 * 2 * TT)
            for s in range(2):
                hb = SB_ // 2
                rows = slot_token[s * hb * BS * NE:(s + 1) * hb * BS * NE]
                pool.dma_start(IDX[0:BS, s * hb * NE:(s + 1) * hb * NE].rearrange("s (b e) -> s b e", e=NE),
                               rows.rearrange("(b s e) o -> s b (e o)", s=BS, e=NE)).then_inc(y_out[s].h, 16)
            for s in y_out:
                pool.wait_ge(s.h, 16)
            done(pool, pool.tensor_scalar(GIDX[0:BS, :], IDX[0:BS, :], T, -T, ALU.is_ge, ALU.mult), rows_known)
            done(pool, pool.tensor_tensor(GIDX[0:BS, :], IDX[0:BS, :], GIDX[0:BS, :], ALU.add), rows_known)
            done(pool, pool.tensor_scalar(GIDX[0:BS, :], GIDX[0:BS, :], T - 1, None, ALU.min), rows_known)

        filt_in, dft_in, filt_mm, filt_arg, filt_sin = (
            sem(n) for n in ("filt_in", "dft_in", "filt_mm", "filt_arg", "filt_sin"))
        taps_mm, taps_done, energy_mm, energy_root, spec_mm, spec_done = (
            sem(n) for n in ("taps_mm", "taps_done", "energy_mm", "energy_root", "spec_mm", "spec_done"))
        TM = TMP[:].rearrange("p a n -> p (a n)")
        E1F, SQ, WIN = flat(E1[:]), AV[:, 0, :], MO
        posT, fA, fB, fK = E1F[0:33, 2048:2560], E1F[0:64, 2560:3072], E1F[0:64, 3072:3584], E1F[0:64, 3584:4096]
        FW = E1F[0:64, 0:1216]
        ENERGY = [E1F[:, o:o + 512] for o in (1216, 2048, 2560, 3584)]
        CF, SF = HT[:, 0:4, :], HT[:, 4:8, :]
        PL, MI = MO[:], VN[:].rearrange("p t h d -> p (t h d)")[:, 0:2048].rearrange("p (t n) -> p t n", t=TT)
        HRe, HIm = E1[:, 0:4, :], E1[:, 4:8, :]

        @block.sync
        def _(sp):
            sp.wait_ge(wo_ready.h, 8)
            sp.dma_start(CF, dft[0].rearrange("(s p) k -> p s k", p=P)).then_inc(dft_in.h, 16)
            sp.dma_start(SF, dft[1].rearrange("(s p) k -> p s k", p=P)).then_inc(dft_in.h, 16)
            sp.dma_start(WIN[:], window.rearrange("(s p) k -> p s k", p=P)).then_inc(filt_in.h, 16)
            sp.wait_ge(logits_ready.h, 1)
            sp.dma_start(posT, posz).then_inc(filt_in.h, 16)
            sp.dma_start(FW, filt_w).then_inc(filt_in.h, 16)

        def filter_pe(pe, piece):
            if piece == 0:
                pe.wait_ge(filt_in.h, 48)
                pe.wait_ge(dft_in.h, 32)
                for l in range(3):
                    src = (posT, fB, fB)[l]
                    if l:
                        pe.wait_ge(filt_sin.h, l)
                    rows = 33 if l == 0 else 64
                    filt_mm.up(pe.matmul(PS[0:64, 0, :], FW[0:rows, 64 * l:64 * l + 64], src, start=True, stop=True))
                pe.wait_ge(filt_sin.h, 3)
            elif piece == 1:
                for t in range(TT):
                    if t >= 2:
                        pe.wait_ge(taps_done.h, t - 1)
                    for q in range(2):
                        m = pe.matmul(PS[:, 2 + 2 * (t % 2) + q, :], fB[:, t * P:(t + 1) * P],
                                      FW[:, 192 + 512 * q:192 + 512 * (q + 1)], start=True, stop=True)
                    taps_mm.up(m)
                for t in range(TT):
                    pe.wait_ge(taps_done.h, t + 1)
                    m = pe.matmul(PS[:, 1, :], ones, ENERGY[t], start=t == 0, stop=t == TT - 1)
                energy_mm.up(m)
                pe.wait_ge(energy_root.h, 1)
            else:
                for k in (2 * piece - 4, 2 * piece - 3):
                    for q, (mat, src) in enumerate(((CF, PL), (SF, MI))):
                        n = 2 * k + q
                        if n >= 2:
                            pe.wait_ge(spec_done.h, n - 1)
                        for s in range(TT):
                            m = pe.matmul(PS[:, 6 + q, :], mat[:, s, k * P:(k + 1) * P], src[:, s, :],
                                          start=s == 0, stop=s == TT - 1)
                        spec_mm.up(m)
                pe.wait_ge(spec_done.h, 4 * piece - 4)

        MAGIC = 1.5 * 2.0 ** 23
        TWO_PI_HI, TWO_PI_LO = 6.28125, 2.0 * np.pi - 6.28125

        def filter_dve(dve, piece):
            if piece == 0:
                for l in range(3):
                    dve.wait_ge(filt_mm.h, l + 1)
                    done(dve, dve.tensor_scalar(fA, PS[0:64, 0, :], col("filt_b", l, 64), col("filt_freq", 0, 64),
                                                ALU.add, ALU.mult), vchain)
                    done(dve, dve.tensor_scalar(fK, fA, float(1 / (2 * np.pi)), MAGIC, ALU.mult, ALU.add), vchain)
                    done(dve, dve.tensor_scalar(fK, fK, -MAGIC, None, ALU.add), vchain)
                    done(dve, dve.scalar_tensor_tensor(fA, fK, -TWO_PI_HI, fA, ALU.mult, ALU.add), vchain)
                    done(dve, dve.scalar_tensor_tensor(fA, fK, -TWO_PI_LO, fA, ALU.mult, ALU.add), vchain)
                    done(dve, dve.tensor_scalar(fA, fA, 3.1415925, -3.1415925, ALU.min, ALU.max), filt_arg)
            elif piece == 1:
                for t in range(TT):
                    dve.wait_ge(taps_mm.h, t + 1)
                    b = 2 + 2 * (t % 2)
                    done(dve, dve.tensor_tensor(MI[:, t, :], PS[:, b + 1, :], WIN[:, t, :], ALU.mult), vchain)
                    done(dve, dve.tensor_tensor(PL[:, t, :], PS[:, b, :], WIN[:, t, :], ALU.mult), vchain)
                    if t == 0:
                        done(dve, dve.memset(MI[0:1, 0, :], 0.0), vchain)
                    e = ENERGY[t]
                    done(dve, dve.tensor_tensor(e, PL[:, t, :], MI[:, t, :], ALU.add), vchain)
                    done(dve, dve.tensor_tensor(MI[:, t, :], PL[:, t, :], MI[:, t, :], ALU.subtract), vchain)
                    done(dve, dve.tensor_copy(PL[:, t, :], e), vchain)
                    done(dve, dve.tensor_tensor(SQ, MI[:, t, :], MI[:, t, :], ALU.mult), vchain)
                    done(dve, dve.tensor_tensor(e, e, e, ALU.mult), vchain)
                    done(dve, dve.tensor_tensor(e, e, SQ, ALU.add), taps_done)
                dve.wait_ge(energy_root.h, 1)
                done(dve, dve.reciprocal(SQ, SQ), vchain)
            else:
                for k in (2 * piece - 4, 2 * piece - 3):
                    for q in range(2):
                        dve.wait_ge(spec_mm.h, 2 * k + q + 1)
                        spec_done.up(dve.tensor_tensor((HRe, HIm)[q][:, k, :], PS[:, 6 + q, :], SQ, ALU.mult))

        def filter_act(act, piece):
            if piece == 0:
                for l in range(3):
                    act.wait_ge(filt_arg.h, l + 1)
                    filt_sin.up(act.activation(fB, fA, ACT.Sin))
            elif piece == 1:
                act.wait_ge(energy_mm.h, 1)
                energy_root.up(act.activation(SQ, PS[:, 1, :], ACT.Sqrt, bias=eps, scale=0.5))

        PARTS = ((0, 4), (4, 6), (6, 8), (8, 10), (10, None))

        pairs_of = {}

        XG = HR[0:BS, 0:2, :]
        YR = HR[0:BS, 2:4, :]
        XE = ROWS[:, 0:2, :].rearrange("p s (k n) -> p s k n", k=KD)
        HID = ROWS[:, 2, :].rearrange("p (s f n) -> p s f n", s=2, f=4)
        HIDN, SG = (HR[BS:, a, :].rearrange("p (s n) -> p s n", s=2) for a in range(2))
        hid_turned, hid_placed = sem("hid_turned"), sem("hid_placed")
        xg_in = [sem("xg_in0"), sem("xg_in1")]
        idx_picked, xg_turned, xe_placed, gu_ready, sg_done, hid_done, y_ready, y_act, y_dve = (
            sem(n) for n in ("idx_picked", "xg_turned", "xe_placed", "gu_ready", "sg_done", "hid_done", "y_ready",
                             "y_act", "y_dve"))
        rows_picked, g_held, s_held = sem("rows_picked"), sem("g_held"), sem("s_held")
        @block.sync
        def _(sp):
            def again(i, s):
                return [[(gu_ready, 2 * i + 1 + s)], [(gu_ready, 2 * i + 1 + s)], [(y_ready, 2 * i + 1 + s)]]

            with sp.Fori(0, NE // 2 - 1) as i:
                for s in range(2):
                    load_expert(sp, s, 2 * i + 2 + s, again(i, s))
            sp.wait_ge(step_ready.h, 1)
            pairs = sp.value_load(STEP[0:1, 2 * NSTEP:2 * NSTEP + 1], min_val=17, max_val=24)
            pairs_of["sp"] = pairs
            more = sp.value_load(STEP[0:1, 2 * NSTEP + 1:2 * NSTEP + 2], min_val=16, max_val=23)
            with sp.Fori(NE // 2 - 1, more) as i:
                for s in range(2):
                    e = sp.value_load(STEP[0:1, bass.ds(2 * i + 2 + s, 1)], min_val=0, max_val=NE - 1)
                    load_expert(sp, s, e, again(i, s))

        @block.gpsimd
        def _(pool):
            pool.wait_ge(step_ready.h, 1)
            pool.wait_ge(h_out.h, 64)
            pairs = pool.value_load(STEP[0:1, 2 * NSTEP:2 * NSTEP + 1], min_val=17, max_val=24)

            def hold(pool, held, before):
                if not isinstance(before, int) or before > 0:
                    pool.wait_ge(held.h, before)
                a = small[0:1, 6 + (held is s_held), 0:1]
                pool.tensor_tensor(a, ones[0:1, 0:1], ones[0:1, 0:1], ALU.add).then_inc(held.h, 1)

            def gather(s, picked, turned, before):
                pool.wait_ge(idx_picked.h, picked)
                if turned is not None:
                    pool.wait_ge(xg_turned.h, turned)
                hold(pool, g_held, before)
                pool.indirect_dma_start(XG[:, s, :], None, h_rows,
                                        bass.IndirectOffsetOnAxis(ap=XI[0:BS, s:s + 1], axis=0)).then_inc(xg_in[s].h, 16)

            def scatter(s, ready, before):
                pool.wait_ge(y_act.h, ready)
                pool.wait_ge(y_dve.h, ready)
                hold(pool, s_held, before)
                pool.indirect_dma_start(y_rows, bass.IndirectOffsetOnAxis(ap=SI[0:BS, s:s + 1], axis=0),
                                        YR[:, s, :], None).then_inc(y_out[s].h, 16)

            hold(pool, s_held, 0)
            for s in range(2):
                pool.tensor_copy(XI[0:BS, s:s + 1], GIDX[0:BS, s:s + 1]).then_inc(idx_picked.h, 1)
                gather(s, s + 1, None, s)
                pool.tensor_copy(SI[0:BS, s:s + 1], IDX[0:BS, s:s + 1]).then_inc(rows_picked.h, 1)
            more = pool.value_load(STEP[0:1, 2 * NSTEP + 1:2 * NSTEP + 2], min_val=16, max_val=23)
            with pool.Fori(0, more) as i:
                for s in range(2):
                    c = pool.value_load(STEP[0:1, bass.ds(NSTEP + 2 * i + 2 + s, 1)], min_val=0, max_val=SB_ * NE - 1)
                    pool.wait_ge(xg_in[s].h, 16 * i + 16)
                    pool.tensor_copy(XI[0:BS, s:s + 1], GIDX[0:BS, bass.ds(c, 1)]).then_inc(idx_picked.h, 1)
                    gather(s, 2 * i + s + 3, 2 * i + s + 1, 2 * i + s + 2)
                    pool.wait_ge(rows_picked.h, 2 * i + s + 1)
                    scatter(s, 2 * i + s + 3, 2 * i + s + 1)
                    pool.wait_ge(y_out[s].h, 16 * i + 32)
                    pool.tensor_copy(SI[0:BS, s:s + 1], IDX[0:BS, bass.ds(c, 1)]).then_inc(rows_picked.h, 1)
            gather(0, 2 * pairs, 2 * more + 1, 2 * more + 2)
            pool.wait_ge(xg_in[0].h, 16 * pairs + 16)
            pool.wait_ge(rows_picked.h, 2 * pairs)
            for s in range(2):
                scatter(s, 2 * pairs + s + 1, 2 * more + s + 1)
                pool.wait_ge(y_out[s].h, 16 * pairs + 16)

        @block.tensor
        def _(pe):
            pe.wait_ge(dest_ready.h, 1)
            pe.wait_ge(step_ready.h, 1)
            pairs = pe.value_load(STEP[0:1, 2 * NSTEP:2 * NSTEP + 1], min_val=17, max_val=24)

            def turn(s, arrived_rows):
                pe.wait_ge(xg_in[s].h, arrived_rows)
                pe.matmul(PS[:, 4 + s, 0:BS], XG[:, s, 0:P], ident[0:BS, 0:BS], start=True, stop=True)
                for k in range(1, KD):
                    m = pe.transpose(PS[:, 4 + s, BS * k:BS * (k + 1)], XG[:, s, k * P:(k + 1) * P],
                                     ident[0:BS, 0:BS])
                m.then_inc(xg_turned.h, 1)

            turn(0, 16)
            for piece, (a, b) in enumerate(PARTS):
                with pe.Fori(a, b or pairs) as i:
                    for s in range(2):
                        n_gate, n_up, n_down = expert_slots(s)
                        pe.wait_ge(xe_placed.h, 2 * i + s + 1)
                        pe.wait_ge(hid_done.h, 2 * i + s + 1)
                        for n in (n_gate, n_up):
                            pe.wait_ge(slot_in[n].h, before_moe[n] + 16 * i + 16)
                        for k in range(KD):
                            for q, n in enumerate((n_gate, n_up)):
                                w = W[:, n, :].rearrange("p (k c) -> p k c", c=CW)
                                m = pe.matmul(PS[BS * q:BS * (q + 1), s, :], XE[:, s, k, :], w[:, k, :],
                                              start=k == 0, stop=k == KD - 1)
                        m.then_inc(gu_ready.h, 1)
                        turn(1 - s, 16 * i + 16 + 16 * s)
                        pe.wait_ge(hid_done.h, 2 * i + s + 3)
                        half = ident[BS:, BS:]
                        pe.matmul(PS[:, 6 + s, 0:BS], HIDN[:, s, 0:P], half, start=True, stop=True)
                        for f in range(1, 4):
                            m = pe.transpose(PS[:, 6 + s, BS * f:BS * (f + 1)], HIDN[:, s, f * P:(f + 1) * P], half)
                        m.then_inc(hid_turned.h, 1)
                        pe.wait_ge(slot_in[n_down].h, before_moe[n_down] + 16 * i + 16)
                        pe.wait_ge(y_act.h, 2 * i + s + 1)
                        pe.wait_ge(y_dve.h, 2 * i + s + 1)
                        pe.wait_ge(hid_placed.h, 2 * i + s + 1)
                        w = W[:, n_down, :].rearrange("p (k c) -> p k c", c=D)
                        for f in range(4):
                            for c in range(2):
                                m = pe.matmul(PS[BS * c:BS * (c + 1), 2 + s, :], HID[:, s, f, :],
                                              w[:, f, 512 * c:512 * (c + 1)], start=f == 0, stop=f == 3)
                        m.then_inc(y_ready.h, 1)
                if b:
                    pe.wait_ge(y_act.h, 2 * b + 2)
                    pe.wait_ge(y_dve.h, 2 * b + 2)
                    filter_pe(pe, piece)

        @block.scalar
        def _(act):
            act.wait_ge(step_ready.h, 1)
            act.activation(small[:, 0, 0:1], small[:, 2, 0:1], ACT.Copy).then_inc(y_act.h, 2)
            pairs = act.value_load(STEP[0:1, 2 * NSTEP:2 * NSTEP + 1], min_val=17, max_val=24)
            for piece, (a, b) in enumerate(PARTS):
                with act.Fori(a, b or pairs) as i:
                    for s in range(2):
                        act.wait_ge(gu_ready.h, 2 * i + s + 1)
                        act.activation(SG[:, s], PS[0:BS, s, :], ACT.Silu).then_inc(sg_done.h, 1)
                        act.wait_ge(hid_turned.h, 2 * i + s + 1)
                        act.activation(HID[:, s], PS[:, 6 + s, 0:4 * BS].rearrange("p (f n) -> p f n", f=4),
                                       ACT.Copy).then_inc(hid_placed.h, 1)
                        act.wait_ge(y_ready.h, 2 * i + s + 1)
                        act.wait_ge(y_out[s].h, 16 * i + 16)
                        act.activation(YR[:, s, 0:512], PS[0:BS, 2 + s, :], ACT.Copy).then_inc(y_act.h, 1)
                if b:
                    filter_act(act, piece)

        @block.vector
        def _(dve):
            dve.memset(small[:, 1, 0:1], 0.0).then_inc(hid_done.h, 2)
            dve.memset(small[:, 1, 1:2], 0.0).then_inc(y_dve.h, 2)
            pairs = dve.value_load(STEP[0:1, 2 * NSTEP:2 * NSTEP + 1], min_val=17, max_val=24)
            pairs_of["dve"] = pairs

            def place(s, turned):
                dve.wait_ge(xg_turned.h, turned)
                dve.tensor_tensor(XE[:, s], PS[:, 4 + s, :].rearrange("p (k n) -> p k n", k=KD),
                                  spread(colw("norm2"), BS), ALU.mult).then_inc(xe_placed.h, 1)

            place(0, 1)
            for piece, (a, b) in enumerate(PARTS):
                with dve.Fori(a, b or pairs) as i:
                    for s in range(2):
                        dve.wait_ge(sg_done.h, 2 * i + s + 1)
                        dve.tensor_tensor(HIDN[:, s], PS[BS:, s, :], SG[:, s], ALU.mult).then_inc(hid_done.h, 1)
                        place(1 - s, 2 * i + s + 2)
                        dve.wait_ge(y_ready.h, 2 * i + s + 1)
                        dve.wait_ge(y_out[s].h, 16 * i + 16)
                        dve.tensor_copy(YR[:, s, 512:], PS[BS:, 2 + s, :]).then_inc(y_dve.h, 1)
                if b:
                    filter_dve(dve, piece)

        G = W[:, 4:6, :].rearrange("p s n -> p (s n)")
        RING = 4
        w2 = w_in2[0]
        stream2 = [("ctx_qk", w_block(w2, 1536)), ("ctx_v", w_block(w2, 2048))]
        stream2 += [("hy", w_block(w2, 512 * j)) for j in range(3)]
        stream2 += [("qk", w_block(w2, 1536)), ("v", w_block(w2, 2048)), ("og", w_block(w2, 2560))]
        stream2 += [("out", w_block(w_out2[0], 512 * j)) for j in range(2)]
        stream2 += [("up", w_block(w_mlp1[0], 512 * j)) for j in range(8)]
        stream2 += [("down", w_block(w_mlp2[0, D * (j % 4):D * (j % 4 + 1), :], 512 * (j // 4))) for j in range(8)]
        slot2_in = [sem(f"slot2_in{n}") for n in range(RING)]

        def slot2(n):
            return W[:, n % RING, :].rearrange("p (k c) -> p k c", c=CW)

        def arrived2(eng, n):
            eng.wait_ge(slot2_in[n % RING].h, 16 * (n // RING + 1))

        CN = flat(AV[:]).rearrange("p (t n) -> p t n", t=2)
        HC = flat(MO[:]).rearrange("p (k n) -> p k n", k=KD)
        ctx_in = sem("ctx_in")

        def load2(sp, n):
            sp.dma_start(slot2(n), stream2[n][1]).then_inc(slot2_in[n % RING].h, 16)

        @block.sync
        def _(sp):
            sp.wait_ge(spec_done.h, 8)
            sp.dma_start(CN, ctx[0].rearrange("(t p) n -> p t n", p=P)).then_inc(ctx_in.h, 16)
            sp.wait_ge(gu_ready.h, 2 * pairs_of["sp"])
            for n in range(2):
                load2(sp, n)

        @block.vector
        def _(dve):
            for q, name, j, c in ((0, "norm_mix", 8, 0), (1, "norm_mix", 8, 1), (4, "norm_mlp", 32, 0)):
                done(dve, dve.tensor_scalar(small[:, q, 0:8], MOD[:, j:j + 8, c], 1.0, None, ALU.add), vchain)
                done(dve, dve.tensor_tensor(small[:, q, 0:8], small[:, q, 0:8], colw(name), ALU.mult), vchain)

        norm_and_turn(small[:, 1, 0:8], HC, lambda eng, t: eng.wait_ge(ctx_in.h, 16), keep=CN, shift=MOD[:, 0:8, 1],
                      src=CN, tiles=2, squares=MI[:, 0:2, :].rearrange("p a n -> p (a n)"), stat0=2)
        ctx_placed = x_placed.n

        YG = [QK[:, 0:2, :], QK[:, 2:4, :], QK[:, 4:6, :], QK[:, 6:8, :]]
        yg_in = x_in
        x2_done = sem("x2_done")

        @block.sync
        def _(sp):
            for s in range(2):
                sp.wait_ge(y_out[s].h, 16 * pairs_of["sp"] + 16)
            for t in range(TT):
                for q in range(2):
                    n = 2 * t + q
                    if n == 4:
                        load2(sp, 2)
                        load2(sp, 3)
                    if n >= 4:
                        sp.wait_ge(x2_done.h, n - 3)
                    sp.dma_start(YG[n % 4].rearrange("p a n -> p (a n)"),
                                 y_rows[q * T + t * P:q * T + (t + 1) * P, :]).then_inc(yg_in[n % 4].h, 16)

        @block.vector
        def _(dve):
            for t in range(TT):
                for q in range(2):
                    n = 2 * t + q
                    dve.wait_ge(yg_in[n % 4].h, 16 * (n // 4 + 2))
                    done(dve, dve.scalar_tensor_tensor(XN[:, t, :], YG[n % 4].rearrange("p a n -> p (a n)"),
                                                       wk[:, q, t:t + 1], XN[:, t, :], ALU.mult, ALU.add), x2_done)

        prod2 = sem("prod2")
        taken2 = {"act": sem("taken_by_act"), "dve": sem("taken_by_dve")}
        takers = []
        last_group = {}

        def product(pe, who, terms, rows=P, width=512, chunk=None):
            g = len(takers)
            if g >= 4:
                w = takers[g - 4]
                pe.wait_ge(taken2[w].h, sum(x == w for x in takers[:g - 3]))
            for n, (a, b) in enumerate(terms):
                m = pe.matmul(PS[0:rows, g % 4, 0:width], a, b, start=n == 0, stop=n == len(terms) - 1)
            prod2.up(m)
            takers.append(who)
            if chunk is not None:
                last_group[chunk] = g
            return g

        def group(eng, g):
            eng.wait_ge(prod2.h, g + 1)
            return PS[:, g % 4, :]

        kcT = G[:, 0:512].rearrange("p (m n) -> p m n", m=2)
        LGc, EXc, PRc = (G[:, o:o + 1024].rearrange("p (q n) -> p q n", q=4) for o in (512, 2560, 3584))
        GLc = G[0:16, 1536:2048].rearrange("p (d n) -> p d n", d=2)
        GW = G[0:16, 6144:6656]
        kNc = G[:, 4608:5632].rearrange("p (d t n) -> p d t n", d=2, t=2)
        vNc = G[:, 7168:8192].rearrange("p (t n) -> p t n", t=2)
        one_row_c = G[:, 6656:6912]
        S0 = TM[:, 1024:1536].rearrange("p (d m n) -> p d m n", d=2, m=2)
        mask0 = CONST["causal_neg"][0]
        gk_in, masks_in, reset_in = sem("gk_in"), sem("masks_in"), sem("reset_in")

        @block.sync
        def _(sp):
            sp.dma_start(GW, gk_w).then_inc(gk_in.h, 16)
            sp.wait_ge(ranks_ready.h, 1)
            sp.dma_start(C[:, mask0:mask0 + 256], consts2[:, 0:256]).then_inc(masks_in.h, 16)

        gl0 = WS["gk_low"][0]
        cg, ck, cv, cz = [], [], [], []
        ctx_lg, ctx_exp = sem("ctx_lg"), sem("ctx_exp")

        @block.tensor
        def _(pe):
            pe.wait_ge(spec_done.h, 8)
            pe.wait_ge(x_placed.h, ctx_placed)
            for d in range(2):
                cg.append(product(pe, "act", [(WSM[:, gl0 + 32 * k + 16 * d:gl0 + 32 * k + 16 * d + 16], HC[:, k, :])
                                              for k in range(KD)], rows=16, width=CTX))
            arrived2(pe, 0)
            for m in range(2):
                ck.append(product(pe, "act", [(slot2(0)[:, k, 256 + m * P:256 + (m + 1) * P], HC[:, k, :])
                                              for k in range(KD)], width=CTX, chunk=0))
            arrived2(pe, 1)
            for t in range(2):
                cv.append(product(pe, "act", [(HC[:, k, t * P:(t + 1) * P], slot2(1)[:, k, :]) for k in range(KD)],
                                  chunk=1))
            pe.wait_ge(gk_in.h, 16)
            pe.wait_ge(taken2["act"].h, 2)
            for d in range(2):
                for m in range(2):
                    cz.append(product(pe, "dve", [(GW[:, 256 * d + P * m:256 * d + P * (m + 1)], GLc[:, d, :])],
                                      width=CTX))

        @block.scalar
        def _(act):
            for d in range(2):
                b = group(act, cg[d])
                i = act.activation(GLc[:, d, :], b[0:16, 0:CTX], ACT.Copy)
                taken2["act"].up(i)
            for m in range(2):
                taken2["act"].up(act.activation(kcT[:, m, :], group(act, ck[m])[:, 0:CTX], ACT.Copy))
            for t in range(2):
                taken2["act"].up(act.activation(vNc[:, t, :], group(act, cv[t]), ACT.Copy))

        MIXT = QK
        def x2_rows(eng, t):
            eng.wait_ge(x2_done.h, 8)

        norm_and_turn(small[:, 0, 0:8], MIXT, x2_rows, shift=MOD[:, 0:8, 0])

        def gate_logs(lgt, ext, ready):
            taken = taken2["dve"].n

            @block.scalar
            def _(act):
                act.wait_ge(taken2["dve"].h, taken)
                done(act, act.activation(ext, lgt, ACT.Abs), achain)
                done(act, act.activation(ext, ext, ACT.Exp, scale=-1.0), achain)
                ready.up(act.activation(ext, ext, ACT.Ln, bias=1.0))

        @block.vector
        def _(dve):
            done(dve, dve.memset(one_row_c, 1.0), vchain)
            for q in range(4):
                b = group(dve, cz[q])
                taken2["dve"].up(dve.tensor_scalar(LGc[:, q, :], b[:, 0:CTX], col("gk_b", q), None, ALU.add))

        gate_logs(LGc, EXc, ctx_exp)

        @block.vector
        def _(dve):
            dve.wait_ge(ctx_exp.h, 1)
            for q in range(4):
                done(dve, dve.scalar_tensor_tensor(LGc[:, q, :], LGc[:, q, :], 0.0, EXc[:, q, :], ALU.min,
                                                   ALU.subtract), vchain)
            done(dve, dve.tensor_scalar(LGc, LGc, 1.0 / 16, None, ALU.mult), vchain)
            for q in range(4):
                done(dve, dve.tensor_tensor_scan(PRc[:, q, :], one_row_c, LGc[:, q, :], 0.0, ALU.mult, ALU.add),
                     vchain)
            for m in range(2):
                done(dve, dve.tensor_scalar(EXc[:, m, :], PRc[:, m, :], -1.0, PRc[:, m, CTX - 1:CTX], ALU.mult,
                                            ALU.add), vchain)
                done(dve, dve.tensor_tensor(EXc[:, 2 + m, :], PRc[:, 2 + m, :], LGc[:, 2 + m, :], ALU.subtract),
                     ctx_lg)

        @block.scalar
        def _(act):
            act.wait_ge(ctx_lg.h, 2)
            ctx_exp.up(act.activation(EXc, EXc, ACT.Exp))

        ctx_keys, ctx_turned, ctx_kn, ctx_state, s0_kept = (
            sem(n) for n in ("ctx_keys", "ctx_turned", "ctx_kn", "ctx_state", "s0_kept"))

        @block.vector
        def _(dve):
            dve.wait_ge(ctx_exp.h, 2)
            for d in range(2):
                ctx_keys.up(dve.tensor_tensor(EXc[:, 2 * d:2 * d + 2, :], EXc[:, 2 * d:2 * d + 2, :], kcT, ALU.mult))

        X0, U = MI, MO
        UN = ROWS
        hy = []
        conv2 = sem("conv2")

        @block.tensor
        def _(pe):
            pe.wait_ge(x_placed.h, x_placed.n)
            for c in range(3):
                arrived2(pe, 2 + c)
                for j in range(4):
                    hy.append(product(pe, "dve", [(slot2(2 + c)[:, k, j * P:(j + 1) * P], MIXT[:, k, :])
                                                  for k in range(KD)], chunk=2 + c))
            for d in range(2):
                pe.wait_ge(ctx_keys.h, d + 1)
                for t in range(2):
                    for m in range(2):
                        i = pe.transpose(PS[:, 4 + d, (2 * t + m) * P:(2 * t + m + 1) * P],
                                         EXc[:, 2 * d + m, t * P:(t + 1) * P], ident)
                ctx_turned.up(i)
            for d in range(2):
                pe.wait_ge(ctx_kn.h, d + 1)
                for h in range(HEADS):
                    m, r0 = h // 2, 64 * (h % 2)
                    for t in range(2):
                        i = pe.matmul(PS[r0:r0 + 64, 6 + d, m * P:(m + 1) * P], kNc[:, d, t, 64 * h:64 * h + 64],
                                      vNc[:, t, h * P:(h + 1) * P], start=t == 0, stop=t == 1)
                ctx_state.up(i)

        @block.vector
        def _(dve):
            for g in range(12):
                c, j = divmod(g, 4)
                b = group(dve, hy[g])
                dst = (X0[:, j, :], U[:, j, :], TM[:, 0:512])[c]
                src3, dst3 = (a.rearrange("p (r n) -> p r n", n=CHUNK) for a in (b, dst))
                done(dve, dve.tensor_scalar(dst, b, col("conv_w2", 12 + g), col("conv_b2", g), ALU.mult, ALU.add),
                     vchain)
                done(dve, dve.scalar_tensor_tensor(dst3[:, :, 1:], src3[:, :, 0:CHUNK - 1], col("conv_w2", g),
                                                   dst3[:, :, 1:], ALU.mult, ALU.add), vchain)
                done(dve, dve.scalar_tensor_tensor(dst3[:, :, 0:CHUNK - 1], src3[:, :, 1:], col("conv_w2", 24 + g),
                                                   dst3[:, :, 0:CHUNK - 1], ALU.mult, ALU.add), taken2["dve"])
                if c == 2:
                    done(dve, dve.tensor_tensor(U[:, j, :], U[:, j, :], dst, ALU.mult), conv2)
            for d in range(2):
                dve.wait_ge(ctx_turned.h, d + 1)
                ctx_kn.up(dve.tensor_copy(kNc[:, d], PS[:, 4 + d, :].rearrange("p (t n) -> p t n", t=2)))
            for d in range(2):
                dve.wait_ge(ctx_state.h, d + 1)
                done(dve, dve.tensor_copy(S0[:, d], PS[:, 6 + d, 0:256].rearrange("p (m n) -> p m n", m=2)), s0_kept)

        u_turned, un_placed, spec_mul, inv_in = (sem(n) for n in ("u_turned", "un_placed", "spec_mul", "inv_in"))
        fw, gq, gg, gv, gog, inv, gz = [], [], [], [], [], [], []
        qT, kT = (G[:, o:o + 1024].rearrange("p (m n) -> p m n", m=2) for o in (0, 1024))
        LG, QI, KI = (G[:, o:o + 2048].rearrange("p (q n) -> p q n", q=4) for o in (2048, 4096, 6144))
        GL = G[0:16, 4096:5120].rearrange("p (d n) -> p d n", d=2)
        VT, OG = None, None

        @block.tensor
        def _(pe):
            pe.wait_ge(conv2.h, 4)
            pe.wait_ge(ctx_kn.h, 2)
            for t in range(TT):
                if t >= 2:
                    pe.wait_ge(un_placed.h, t - 1)
                for j in range(4):
                    i = pe.transpose(PS[:, 4 + t % 2, j * P:(j + 1) * P], U[:, j, t * P:(t + 1) * P], ident)
                u_turned.up(i)
            pe.wait_ge(un_placed.h, 4)
            for k in range(TT):
                for mat in (CF, SF):
                    fw.append(product(pe, "dve", [(mat[:, s, k * P:(k + 1) * P], UN[:, s, :]) for s in range(TT)]))

        @block.vector
        def _(dve):
            for t in range(TT):
                dve.wait_ge(u_turned.h, t + 1)
                un_placed.up(dve.tensor_copy(UN[:, t, :], PS[:, 4 + t % 2, :]))
            A, B = TM[:, 0:512], TM[:, 512:1024]
            for k in range(TT):
                ur, ui = group(dve, fw[2 * k]), group(dve, fw[2 * k + 1])
                hr, hi = HRe[:, k, :], HIm[:, k, :]
                dve.tensor_tensor(A, ur, hr, ALU.mult).then_inc(vchain.h, 1)
                vchain.n += 1
                done(dve, dve.tensor_tensor(B, ur, hi, ALU.mult), taken2["dve"])
                dve.wait_ge(vchain.h, vchain.n)
                done(dve, dve.tensor_tensor(hr, ui, hr, ALU.mult), vchain)
                done(dve, dve.tensor_tensor(hi, ui, hi, ALU.mult), taken2["dve"])
                done(dve, dve.tensor_tensor(hi, A, hi, ALU.subtract), vchain)
                done(dve, dve.tensor_tensor(hr, B, hr, ALU.add), spec_mul)

        ke_turned, kn_placed = sem("ke_turned"), sem("kn_placed")
        logs_ready, hy_done, b_ready, b_exp, keys_ready = (
            sem(n) for n in ("logs_ready", "hy_done", "b_ready", "b_exp", "keys_ready"))

        @block.tensor
        def _(pe):
            for d in range(2):
                gg.append(product(pe, "act", [(WSM[:, gl0 + 32 * k + 16 * d:gl0 + 32 * k + 16 * d + 16],
                                               MIXT[:, k, :]) for k in range(KD)], rows=16))
            low_taken = sum(w == "act" for w in takers)
            arrived2(pe, 5)
            for j in range(4):
                gq.append(product(pe, "act", [(slot2(5)[:, k, j * P:(j + 1) * P], MIXT[:, k, :]) for k in range(KD)],
                                  chunk=5))
            pe.wait_ge(taken2["act"].h, low_taken)
            for d in range(2):
                for m in range(2):
                    gz.append(product(pe, "dve", [(GW[:, 256 * d + P * m:256 * d + P * (m + 1)], GL[:, d, :])]))
            pe.wait_ge(inv_in.h, 32)
            pe.wait_ge(spec_mul.h, 4)
            for j in range(4):
                c = slice(j * P, (j + 1) * P)
                inv.append(product(pe, "dve", [(HIm[:, k, c], CF[:, k, :]) for k in range(TT)] +
                                              [(HRe[:, k, c], SF[:, k, :]) for k in range(TT)]))
            arrived2(pe, 6)
            for t in range(TT):
                gv.append(product(pe, "act", [(MIXT[:, k, t * P:(t + 1) * P], slot2(6)[:, k, :]) for k in range(KD)],
                                  chunk=6))
            pe.wait_ge(keys_ready.h, 2)
            pe.wait_ge(un_placed.h, 4)
            for d in range(2):
                for tp in range(2):
                    for t in range(2):
                        for m in range(2):
                            tt = 2 * tp + t
                            i = pe.transpose(PS[:, 4 + 2 * d + tp, (2 * t + m) * P:(2 * t + m + 1) * P],
                                             LG[:, 2 * d + m, tt * P:(tt + 1) * P], ident)
                    ke_turned.up(i)
            arrived2(pe, 7)
            for j in range(4):
                gog.append(product(pe, "act", [(slot2(7)[:, k, j * P:(j + 1) * P], MIXT[:, k, :]) for k in range(KD)],
                                   chunk=7))

        VT, OG = HT[:, 4:8, :], ROWS
        AV0 = AV[:, 0, :]

        @block.scalar
        def _(act):
            act.wait_ge(s0_kept.h, 2)
            for d in range(2):
                taken2["act"].up(act.activation(GL[:, d, :], group(act, gg[d])[0:16, :], ACT.Copy))
            for j in range(4):
                dst = (qT, kT)[j // 2][:, j % 2, :]
                taken2["act"].up(act.activation(dst, group(act, gq[j]), ACT.Copy, scale=64 ** -0.5 if j < 2 else 1.0))

        @block.vector
        def _(dve):
            for q in range(4):
                taken2["dve"].up(dve.tensor_scalar(LG[:, q, :], group(dve, gz[q]), col("gk_b", q), None, ALU.add))

        gate_logs(LG, QI, logs_ready)
        Lt, DEC = rs, ss

        @block.vector
        def _(dve):
            dve.wait_ge(logs_ready.h, 1)
            done(dve, dve.scalar_tensor_tensor(flat(LG), flat(LG), 0.0, flat(QI), ALU.min, ALU.subtract), vchain)
            done(dve, dve.tensor_scalar(LG, LG, 1.0 / 16, None, ALU.mult), vchain)
            dve.wait_ge(reset_in.h, 16)
            for q in range(4):
                done(dve, dve.tensor_tensor_scan(KI[:, q, :], AV0, LG[:, q, :], 0.0, ALU.mult, ALU.add), vchain)
            chunks = lambda a: a.rearrange("p q (n c) -> p q n c", c=CHUNK)
            done(dve, dve.tensor_copy(Lt[:], chunks(KI)[:, :, :, CHUNK - 1]), vchain)
            for q in range(4):
                lsp = spread(Lt[:, q, :], CHUNK)
                kc, lc = chunks(KI)[:, q], chunks(LG)[:, q]
                if q >= 2:
                    done(dve, dve.tensor_tensor(lc, lc, kc, ALU.subtract), vchain)
                    done(dve, dve.tensor_tensor(kc, lc, lsp, ALU.add), vchain)
                done(dve, dve.tensor_tensor(lc, lsp, kc, ALU.subtract), b_ready)
            for j in range(4):
                done(dve, dve.scalar_tensor_tensor(U[:, j, :], U[:, j, :], col("hyena_b", j), group(dve, inv[j]),
                                                   ALU.mult, ALU.add), taken2["dve"])
                hy_done.up(dve.tensor_tensor(U[:, j, :], U[:, j, :], X0[:, j, :], ALU.mult))

        @block.scalar
        def _(act):
            act.wait_ge(b_ready.h, 4)
            b_exp.up(act.activation(QI, KI, ACT.Exp))
            b_exp.up(act.activation(LG, LG, ACT.Exp))
            act.wait_ge(b_exp.h, 1)
            b_exp.up(act.activation(KI, KI, ACT.Exp, scale=-1.0))
            b_exp.up(act.activation(DEC[:], Lt[:], ACT.Exp))
            for t in range(TT):
                taken2["act"].up(act.activation(VT[:, t, :], group(act, gv[t]), ACT.Copy))
            for i in range(4):
                act.wait_ge(ke_turned.h, i + 1)
                kn_placed.up(act.activation(HT[:, i, :], PS[:, 4 + i, :], ACT.Copy))
            for j in range(4):
                taken2["act"].up(act.activation(OG[:, j, :], group(act, gog[j]), ACT.Silu))

        @block.vector
        def _(dve):
            for n, (a, b) in enumerate(((LG, kT), (QI, qT), (KI, kT))):
                dve.wait_ge(b_exp.h, 3 if n == 2 else 2)
                for d in range(2):
                    o = a[:, 2 * d:2 * d + 2, :]
                    keys_ready.up(dve.tensor_tensor(o, o, b, ALU.mult))

        KN = HT[:, 0:4, :].rearrange("p (d t) n -> p d (t n)", d=2).rearrange("p d (t n) -> p d t n", t=TT)
        ST = E1[:].rearrange("p a n -> p (a n)").rearrange("p (d c m n) -> p d c m n", d=2, c=8, m=2)
        AM = QK[:, 4:8, :]
        ON = TM.rearrange("p (t n) -> p t n", t=TT)
        MASK = [C[:, mask0 + P * d:mask0 + P * (d + 1)].bitcast(U32) for d in range(2)]
        ds_ready, s_start, am_zero, att_ready, att_masked, o_ready, o_kept = (
            sem(n) for n in ("ds_ready", "s_start", "am_zero", "att_ready", "att_masked",
                             "o_ready", "o_kept"))

        def ds_place(d, n):
            o = 256 * ((n // 2) % 2)
            return PS[:, (4, 0)[d] + 2 * (n % 2) + n // 4, o:o + 256].rearrange("p (m n) -> p m n", m=2)

        @block.tensor
        def _(pe):
            pe.wait_ge(kn_placed.h, 4)
            for w in ("act", "dve"):
                pe.wait_ge(taken2[w].h, sum(x == w for x in takers))
            for d in range(2):
                for n in range(8):
                    t, r = n // 2, 64 * (n % 2)
                    for h in range(HEADS):
                        m, r0 = h // 2, 64 * (h % 2)
                        i = pe.matmul(ds_place(d, n)[r0:r0 + 64, m, :], KN[r:r + 64, d, t, 64 * h:64 * h + 64],
                                      VT[r:r + 64, t, h * P:(h + 1) * P], start=True, stop=True)
                ds_ready.up(i)
            pe.wait_ge(keys_ready.h, 6)
            pe.wait_ge(s_start.h, 32)
            units = [(t, d) for t in range(TT) for d in range(2)]

            def score(u):
                t, d = units[u]
                if u >= 2:
                    pe.wait_ge(att_masked.h, 2 * (u - 1))
                for h in range(HEADS):
                    m, r0 = h // 2, 64 * (h % 2)
                    i = pe.matmul(PS[:, 2 * (u % 2) + h % 2, m * P:(m + 1) * P],
                                  KI[r0:r0 + 64, 2 * d + m, t * P:(t + 1) * P],
                                  QI[r0:r0 + 64, 2 * d + m, t * P:(t + 1) * P], start=True, stop=True)
                att_ready.up(i)

            score(0)
            score(1)
            for t in range(TT):
                for d in range(2):
                    if 2 * t + 2 + d < 8:
                        score(2 * t + 2 + d)
                if t >= 2:
                    pe.wait_ge(o_kept.h, 2 * (t - 1))
                pe.wait_ge(att_masked.h, 4 * (t + 1))
                for h in range(HEADS):
                    m, r0 = h // 2, 64 * (h % 2)
                    bank, o = 4 + 2 * (t % 2) + h % 2, m * P
                    for d in range(2):
                        pe.matmul(PS[:, bank, o:o + P], AM[:, 2 * (t % 2) + d, h * P:(h + 1) * P],
                                  VT[:, t, h * P:(h + 1) * P], start=d == 0, stop=False)
                    for d in range(2):
                        for c in range(2):
                            n = 2 * t + c
                            i = pe.matmul(PS[64 * c:64 * c + 64, bank, o:o + P],
                                          QI[r0:r0 + 64, 2 * d + m, n * CHUNK:(n + 1) * CHUNK],
                                          ST[r0:r0 + 64, d, n, m, :], start=False, stop=d == 1)
                o_ready.up(i)

        @block.vector
        def _(dve):
            dve.wait_ge(prod2.h, gog[-1] + 1)
            am_zero.up(dve.memset(AM, 0.0))
            dve.wait_ge(b_exp.h, 4)
            dve.wait_ge(ds_ready.h, 2)
            for d in range(2):
                for m in range(2):
                    s_start.up(dve.tensor_copy(ST[:, d, 7 * d, m], S0[:, d, m]))
            for i in range(7):
                for d in range(2):
                    n = i if d == 0 else 7 - i
                    for m in range(2):
                        dve.wait_ge(s_start.h, 4 * i + 2 * d + m + 1)
                        s_start.up(dve.scalar_tensor_tensor(ST[:, d, n + 1 - 2 * d, m], ST[:, d, n, m],
                                                            DEC[:, 2 * d + m, n:n + 1], ds_place(d, n)[:, m, :],
                                                            ALU.mult, ALU.add))
            dve.wait_ge(am_zero.h, 1)
            dve.wait_ge(masks_in.h, 16)
            for u in range(8):
                t, d = divmod(u, 2)
                if t >= 2:
                    dve.wait_ge(o_ready.h, t - 1)
                dve.wait_ge(att_ready.h, u + 1)
                for e in range(2):
                    a = AM[:, 2 * (t % 2) + d, :].rearrange("p (m e n) -> p m e n", m=2, e=2)[:, :, e, :]
                    p = PS[:, 2 * (u % 2) + e, 0:256].rearrange("p (m n) -> p m n", m=2)
                    if t >= 2:
                        dve.wait_ge(att_masked.h, 4 * (t - 1))
                    att_masked.up(dve.copy_predicated(a, MASK[d].unsqueeze(1).to_broadcast([P, 2, P]), p))

        @block.scalar
        def _(act):
            for t in range(TT):
                act.wait_ge(o_ready.h, t + 1)
                for e in range(2):
                    o = ON[:, t, :].rearrange("p (m e n) -> p m e n", m=2, e=2)[:, :, e, :]
                    o_kept.up(act.activation(o, PS[:, 4 + 2 * (t % 2) + e, 0:256].rearrange("p (m n) -> p m n", m=2),
                                             ACT.Copy))

        @block.vector
        def _(dve):
            dve.wait_ge(o_kept.h, 8)
            dve.wait_ge(taken2["act"].h, taken2["act"].n)

        @block.tensor
        def _(pe):
            pe.wait_ge(o_kept.h, 8)

        head_norm(ON, "gla_norm", QK[:, 0:4, :], 1.0, sq=flat(AV[:]), gate=OG)

        G1B, G2B, NF, DG = (G[:, D * i:D * (i + 1)] for i in range(4))
        gate_diag, x3_done, nf_in = sem("gate_diag"), sem("x3_done"), sem("nf_in")
        gb, op_ = [], []

        @block.vector
        def _(dve):
            for i in range(2):
                if i:
                    dve.wait_ge(prod2.h, gog[-1] + 3)
                for j in range(KD):
                    gate_diag.up(dve.tensor_scalar(DG[:, j * P:(j + 1) * P], ident, MOD[:, (16, 40)[i] + j, 0:1], None,
                                                   ALU.mult))

        @block.tensor
        def _(pe):
            pe.wait_ge(att_masked.h, 16)
            for i in range(2):
                pe.wait_ge(gate_diag.h, 8 * i + 8)
                for c in range(2):
                    gb.append(product(pe, "act", [(ones, DG[:, 512 * c:512 * (c + 1)])]))
            pe.wait_ge(head_placed.h, 12)
            pe.wait_ge(hy_done.h, 4)
            for c in range(2):
                arrived2(pe, 8 + c)
                for t in range(TT):
                    op_.append(product(pe, "dve", [((MO if j < 4 else QK)[:, j % 4, t * P:(t + 1) * P],
                                                    slot2(8 + c)[:, j, :]) for j in range(KD)], chunk=8 + c))

        @block.scalar
        def _(act):
            for n, g in enumerate(gb):
                taken2["act"].up(act.activation((G1B, G2B)[n // 2][:, 512 * (n % 2):512 * (n % 2 + 1)], group(act, g),
                                                ACT.Copy))

        gates_taken = taken2["act"].n

        @block.vector
        def _(dve):
            dve.wait_ge(taken2["act"].h, gates_taken)
            dve.wait_ge(head_turned.h, 12)
            for n, g in enumerate(op_):
                c, t = divmod(n, 4)
                cs = slice(512 * c, 512 * (c + 1))
                tmp = TM[:, 512 * (n % 4):512 * (n % 4 + 1)]
                done(dve, dve.tensor_tensor(tmp, group(dve, g), G1B[:, cs], ALU.mult), taken2["dve"])
                x3_done.up(dve.tensor_tensor(XN[:, t, cs], XN[:, t, cs], tmp, ALU.add))
            dve.wait_ge(x3_done.h, 8)

        norm_and_turn(small[:, 4, 0:8], HT, lambda eng, t: eng.wait_ge(x3_done.h, 8), shift=MOD[:, 24:32, 0])
        HIDT = [E1[:, j, :] for j in range(8)] + [QK[:, j, :] for j in range(8)]
        HIDT += [MI[:, j, :] for j in range(4)] + [B[:, j, :] for B in (MO, AV, ROWS) for j in range(4)]
        up, squared, down_mm, x4_done, root, norm4 = (
            [], sem("squared"), sem("down_mm"), sem("x4_done"), sem("last_root"), sem("last_normed"))
        out_done = sem("out_done")

        @block.tensor
        def _(pe):
            pe.wait_ge(x_placed.h, x_placed.n)
            for f in range(32):
                n = 10 + f // 4
                if f % 4 == 0:
                    arrived2(pe, n)
                up.append(product(pe, "act", [(slot2(n)[:, k, (f % 4) * P:(f % 4 + 1) * P], HT[:, k, :])
                                              for k in range(KD)], chunk=n))
            pe.wait_ge(taken2["act"].h, sum(x == "act" for x in takers))
            for c in range(2):
                for r in range(4):
                    n = 18 + 4 * c + r
                    arrived2(pe, n)
                    if c == 0:
                        pe.wait_ge(squared.h, 8 * (r + 1))
                    for t in range(TT):
                        for k in range(KD):
                            i = pe.matmul(PS[:, 4 * c + t, :], HIDT[8 * r + k][:, t * P:(t + 1) * P],
                                          slot2(n)[:, k, :], start=r == 0 and k == 0, stop=r == 3 and k == KD - 1)
                        if t == TT - 1 or (c, r) == (1, 3):
                            down_mm.up(i)

        @block.scalar
        def _(act):
            for f, g in enumerate(up):
                taken2["act"].up(act.activation(HIDT[f], group(act, g), ACT.Relu))

        relu0 = taken2["act"].n - 32

        OUT = flat(HT[:]).rearrange("p (t n) -> p t n", t=TT)

        @block.vector
        def _(dve):
            for f in range(32):
                dve.wait_ge(taken2["act"].h, relu0 + f + 1)
                squared.up(dve.tensor_tensor(HIDT[f], HIDT[f], HIDT[f], ALU.mult))
            def add(c, t):
                cs = slice(512 * c, 512 * (c + 1))
                tmp = TM[:, 512 * t:512 * (t + 1)]
                done(dve, dve.tensor_tensor(tmp, PS[:, 4 * c + t, :], G2B[:, cs], ALU.mult), vchain)
                x4_done.up(dve.tensor_tensor(XN[:, t, cs], XN[:, t, cs], tmp, ALU.add))

            def last_norm(t):
                dve.wait_ge(root.h, t + 1)
                done(dve, dve.reciprocal(rs[:, t, 1:2], rs[:, t, 0:1]), vchain)
                norm4.up(dve.scalar_tensor_tensor(OUT[:, t, :], XN[:, t, :], rs[:, t, 1:2], NF, ALU.mult, ALU.mult))

            dve.wait_ge(down_mm.h, 4)
            for t in range(TT):
                add(0, t)
            dve.wait_ge(nf_in.h, 16)
            for t in range(TT):
                dve.wait_ge(down_mm.h, 8 + t)
                add(1, t)
                if t:
                    last_norm(t - 1)
            last_norm(TT - 1)

        @block.scalar
        def _(act):
            for t in range(TT):
                act.wait_ge(x4_done.h, 5 + t)
                done(act, act.activation(OUT[:, t, :], XN[:, t, :], ACT.Square, accum_out=ss[:, t, 0:1]), achain)
                root.up(act.activation(rs[:, t, 0:1], ss[:, t, 0:1], ACT.Sqrt, bias=eps, scale=1.0 / D))

        @block.sync
        def _(sp):
            for n in range(RING, len(stream2)):
                if n - RING in last_group:
                    sp.wait_ge(prod2.h, last_group[n - RING] + 1)
                else:
                    sp.wait_ge(down_mm.h, n - RING - 18 + 1)
                load2(sp, n)
                if n == 8:
                    sp.wait_ge(prod2.h, fw[-1] + 1)
                    for q, m in enumerate((CF, SF)):
                        sp.dma_start(m, dft[2 + q].rearrange("(s p) k -> p s k", p=P)).then_inc(inv_in.h, 16)
                    sp.dma_start(AV0, consts2[:, 256:768]).then_inc(reset_in.h, 16)
                if n == 12:
                    sp.wait_ge(ke_turned.h, 4)
                    sp.dma_start(NF, norm_final.to_broadcast([P, D])).then_inc(nf_in.h, 16)
            for t in range(TT):
                sp.wait_ge(norm4.h, t + 1)
                sp.dma_start(out[0, t * P:(t + 1) * P, :], OUT[:, t, :]).then_inc(out_done.h, 16)
            sp.wait_ge(out_done.h, 16 * TT)


def layouts(a):
    def tiles(v):
        return v.reshape(-1, P).T

    def head(v, n=1):
        o = np.zeros((P, n), np.float32)
        o[:v.shape[0], :] = v.reshape(v.shape[0], n)
        return o

    c = {
        "norm1": tiles(a["norm1_w"][0]), "conv_w": tiles(a["conv_w"][0].reshape(-1)), "conv_b": tiles(a["conv_b"][0]),
        "m_norm": tiles(a["m_norm_w"][0]), "a_norm": tiles(a["a_norm_w"][0]),
        "q_norm": np.concatenate([a["q_norm_w"][0]] * 2)[:, None],
        "k_norm": np.concatenate([a["k_norm_w"][0]] * 2)[:, None], "norm2": tiles(a["norm2_w"][0]),
        "b_gates": head(np.stack([a["b_igate"][0], a["b_fgate"][0]], 1), 2),
        "lam_a": head(np.stack([a["lambda_q1"][0], a["lambda_q2"][0]], 1), 2),
        "lam_b": head(np.stack([a["lambda_k1"][0], a["lambda_k2"][0]], 1), 2),
        "cvec": np.stack([tiles(a["c_2"][0]), tiles(a["c_ctx_2"])], 2).reshape(P, 16),
        "b_ada": tiles(a["b_ada_2"][0]), "norm_mix": tiles(a["norm_mix_2"][0]), "norm_mlp": tiles(a["norm_mlp_2"][0]),
        "conv_w2": tiles(a["conv_w_2"][0].reshape(-1)), "conv_b2": tiles(a["conv_b_2"][0]),
        "hyena_b": tiles(a["hyena_bias_2"][0]), "gla_norm": tiles(a["gla_norm_2"][0]),
        "gk_b": np.concatenate([tiles(a["gk_b_fwd_2"][0]), tiles(a["gk_b_bwd_2"][0])], 1),
        "filt_b": head(np.stack([a["filt_b1_2"][0], a["filt_b2_2"][0], a["filt_b3_2"][0]], 1), 3),
        "filt_freq": head(a["filt_freq_2"][0]),
    }
    for name, (_, w) in COLS.items():
        assert c[name].shape == (P, w), (name, c[name].shape)
    cols = np.concatenate([c[name] for name in COLS], 1)
    i, j = np.arange(P)[:, None], np.arange(P)[None, :]
    row = lambda v: np.broadcast_to(np.asarray(v, np.float32)[None, :], (P, len(v)))
    e = np.arange(NE)
    k = {
        "ident": i == j, "ones": np.ones((P, P)), "causal_neg": np.where(j >= i, 0.0, -BIG), "before": i < j,
        "group_m8": row(e // EG - 8), "expert_m64": row(e - 64), "expert": row(e),
        "lane_m8": row(np.arange(NG) - 8), "token": np.arange(T).reshape(TT, P).T,
        "block_edge": row(BS * np.arange(1, 8)), "pair_edge": row(2 * np.arange(8)), "extra": row(np.arange(18)),
        "steps": row(np.arange(32)), "eps": np.full((P, 1), EPS),
    }
    consts = np.concatenate([np.asarray(k[name], np.float32) for name in CONST], 1)
    assert consts.shape == (P, NCONST)

    def small(w):
        return w.reshape(KD, P, -1).transpose(1, 0, 2).reshape(P, -1)

    wsmall = np.concatenate([small(a["w_in"][0][:, 2048:2056]),
                             small(np.concatenate([a["w_group"][0], a["w_expert"][0]], 1)),
                             small(a["w_in_2"][0][:, 3072:3104])], 1)
    n = np.arange(T, dtype=np.float64)
    fwd = np.pi * n[:, None] * (2 * n[None, :] + 1) / (2 * T)
    dft = np.stack([np.cos(fwd), -np.sin(fwd), np.cos(fwd.T) / T, -np.sin(fwd.T) / T]).astype(np.float32)
    f32 = np.float32
    pos = np.linspace(0.0, 1.0, T, dtype=f32)[:, None]
    ang = (f32(2.0 * np.pi) * np.arange(T, dtype=f32) / f32(T))[:, None] * np.linspace(1e-4, 15, 16, dtype=f32)[None, :]
    posz = np.ascontiguousarray(np.concatenate([pos, np.cos(ang), -np.sin(ang)], 1).T)
    rates = np.abs(np.linspace(np.log(1e-2) / 1.5, np.log(1e-2) / 0.3, 512, dtype=f32))
    window = np.exp(-pos * rates[None, :]).astype(f32)
    filt_w = np.concatenate([head(a["filt_w1_2"][0], 64)[:64], a["filt_w2_2"][0], a["filt_w3_2"][0],
                             a["filt_wout_2"][0]], 1)
    same = (i // CHUNK) == (j // CHUNK)
    reset = np.broadcast_to((np.arange(T) % CHUNK != 0)[None, :], (P, T))
    consts2 = np.concatenate([same & (i <= j), same & (i >= j), reset], 1).astype(f32)
    return dict(dft=dft, window=window, posz=posz, filt_w=filt_w, consts2=consts2,
                gk_w=np.concatenate([a["gk_w_fwd_2"][0], a["gk_w_bwd_2"][0]], 1), norm_final=a["norm_final_2"][None, :],
                x=a["x"], w_in=a["w_in"], w_out=a["w_out"], w_gate=a["w_gate"], w_up=a["w_up"], w_down=a["w_down"],
                w_ada=a["w_ada_2"], ctx=a["ctx_2"], w_in2=a["w_in_2"], w_out2=a["w_out_2"], w_mlp1=a["w_mlp1_2"],
                w_mlp2=a["w_mlp2_2"], cols=cols, consts=consts, wsmall=wsmall,
                bias36=np.concatenate([a["b_group"], a["b_expert"]], 1))


def kernel(**inputs):
    import concourse.bacc as bacc
    from concourse.bass_utils import run_bass_kernel_spmd

    arrays = {n: np.ascontiguousarray(v) for n, v in layouts({n: np.asarray(v) for n, v in inputs.items()}).items()}
    nc = bacc.Bacc("TRN2", target_bir_lowering=False, num_devices=1)
    args = {n: nc.dram_tensor(n, v.shape, mybir.dt.from_np(v.dtype), kind="ExternalInput").ap()
            for n, v in arrays.items()}
    out = nc.dram_tensor("out", (1, T, D), F32, kind="ExternalOutput").ap()
    mixer_moe_hyena(nc, out=out, **args)
    r = run_bass_kernel_spmd(nc, [arrays], core_ids=[0])
    return r.results[0]["out"]
```
